# Optimizing a Trainium2 kernel written in Bass

```python
import jax, jax.numpy as jnp
from jax import lax
import numpy as np

D_MODEL = 1024
BATCH = 1
SEQ = 512
DEPTH = 1
DEC_BATCH = 1
DEC_SEQ = 32
PAST_LEN = 1024

CHUNK = 64
N_META = 16
D_MIX = D_MODEL
D_HGRN = D_MIX // 2
D_POOL = D_MIX - D_HGRN
H_A = 4
DK = D_HGRN // H_A
DV = D_HGRN // H_A
POOL_WINDOWS = (2, 4, 8, 16)
N_POOL_GROUPS = 4
POOL_GW = D_POOL // N_POOL_GROUPS
POOL_HIST = 15
D_IN_PROJ = 4 * D_HGRN + D_POOL
PEER_HEADS = 8
N_KEYS = 128
N_EXPERTS = N_KEYS * N_KEYS
PEER_DKEY = 256
PEER_TOPK = 16
PEER_BLOCK = 128
EPS = 1e-6

kernel_name = 'hymba_hgrn2_pool_peer_stream_step'

def rmsnorm(x, w):
    xf = x.astype(jnp.float32)
    y = xf * lax.rsqrt(jnp.mean(xf * xf, axis=-1, keepdims=True) + EPS) * w.astype(jnp.float32)
    return y.astype(x.dtype)

def _hgrn2_chunk(S, blk):
    q, k, v, g = blk
    C = q.shape[2]
    b = jnp.cumsum(g, axis=2)
    o_inter = jnp.einsum('bhck,bhkv->bhcv', q * jnp.exp(b), S)
    causal = jnp.tril(jnp.ones((C, C), dtype=bool))
    diff = b[:, :, :, None, :] - b[:, :, None, :, :]
    decay = jnp.exp(jnp.where(causal[:, :, None], diff, -jnp.inf))
    A = jnp.einsum('bhtk,bhsk,bhtsk->bhts', q, k, decay)
    o = o_inter + jnp.einsum('bhts,bhsv->bhtv', A, v)
    b_last = b[:, :, -1, :]
    S_new = jnp.exp(b_last)[..., None] * S + jnp.einsum(
        'bhck,bhcv->bhkv', k * jnp.exp(b_last[:, :, None, :] - b), v)
    return S_new, o

def hgrn2_recurrence(q, k, v, g, S0):
    B, T = q.shape[0], q.shape[1]
    pad = (-T) % CHUNK

    def prep(a):
        a = jnp.pad(a, ((0, 0), (pad, 0), (0, 0), (0, 0)))
        n = a.shape[1] // CHUNK
        return a.reshape(B, n, CHUNK, H_A, a.shape[-1]).transpose(1, 0, 3, 2, 4)

    S, o = lax.scan(_hgrn2_chunk, S0, (prep(q), prep(k), prep(v), prep(g)))
    o = o.transpose(1, 0, 3, 2, 4).reshape(B, -1, H_A, DV)[:, pad:]
    return o, S

def pool_mixer(u_hist, u_new, n_hist, pool_w, pool_scale):
    T = u_new.shape[1]
    u_ext = jnp.concatenate([u_hist, u_new], axis=1)
    uf = u_ext.astype(jnp.float32)
    cs = jnp.pad(jnp.cumsum(uf, axis=1), ((0, 0), (1, 0), (0, 0)))
    avail = n_hist + jnp.arange(T, dtype=jnp.float32) + 1.0
    outs = []
    for gi, w in enumerate(POOL_WINDOWS):
        lo, hi = gi * POOL_GW, (gi + 1) * POOL_GW
        end = cs[:, POOL_HIST + 1:POOL_HIST + 1 + T, lo:hi]
        start = cs[:, POOL_HIST + 1 - w:POOL_HIST + 1 - w + T, lo:hi]
        cnt = jnp.minimum(jnp.float32(w), avail)[None, :, None]
        d = (end - start) / cnt - uf[:, POOL_HIST:, lo:hi]
        outs.append(jnp.einsum('btc,cd->btd', d, pool_w[gi].astype(jnp.float32)))
    out = jnp.concatenate(outs, axis=-1) * pool_scale.astype(jnp.float32)
    return out, u_ext[:, -POOL_HIST:]

def peer_ffn(x, w_query, subkeys, u_tab, v_tab):
    B, T, D = x.shape
    xt = x.reshape(-1, D)
    n = xt.shape[0]
    npad = (-n) % PEER_BLOCK
    blocks = jnp.pad(xt, ((0, npad), (0, 0))).reshape(-1, PEER_BLOCK, D)

    def block_fn(xb):
        q = (xb @ w_query).reshape(PEER_BLOCK, PEER_HEADS, 2, PEER_DKEY // 2)
        s = jnp.einsum('thpd,hpnd->thpn', q, subkeys)
        sv, si = lax.top_k(s, PEER_TOPK)
        cand = (sv[:, :, 0, :, None] + sv[:, :, 1, None, :]).reshape(PEER_BLOCK, PEER_HEADS, -1)
        cidx = (si[:, :, 0, :, None] * N_KEYS + si[:, :, 1, None, :]).reshape(PEER_BLOCK, PEER_HEADS, -1)
        top_s, pos = lax.top_k(cand, PEER_TOPK)
        experts = jnp.take_along_axis(cidx, pos, axis=-1)
        gate = jax.nn.softmax(top_s.astype(jnp.float32), axis=-1)
        u = jnp.take(u_tab, experts, axis=0)
        a = jax.nn.gelu(jnp.einsum('td,thkd->thk', xb, u).astype(jnp.float32), approximate=False)
        v = jnp.take(v_tab, experts, axis=0)
        return jnp.einsum('thk,thkd->td', (gate * a).astype(xb.dtype), v)

    ys = lax.map(block_fn, blocks)
    return ys.reshape(-1, D)[:n].reshape(B, T, D).astype(x.dtype)

def trunk_layer(h, S0, pool_hist, n_hist, lb, norm_mix, w_in, out_norm, pool_w, pool_scale,
                w_out, norm_ffn, peer_w_query, peer_subkeys, peer_u, peer_v):
    B, T, _ = h.shape
    xn = rmsnorm(h, norm_mix)
    proj = xn @ w_in
    zq, zf, zi, zg, zp = jnp.split(proj, [D_HGRN, 2 * D_HGRN, 3 * D_HGRN, 4 * D_HGRN], axis=-1)
    q = (jax.nn.silu(zq.astype(jnp.float32)) * DK ** -0.5).reshape(B, T, H_A, DK)
    zf = zf.astype(jnp.float32)
    log_f = jnp.log(lb + (1.0 - lb) * jax.nn.sigmoid(zf)).reshape(B, T, H_A, DK)
    k = ((1.0 - lb) * jax.nn.sigmoid(-zf)).reshape(B, T, H_A, DK)
    v = zi.astype(jnp.float32).reshape(B, T, H_A, DV)
    o, S_new = hgrn2_recurrence(q, k, v, log_f, S0.astype(jnp.float32))
    o = o * lax.rsqrt(jnp.mean(o * o, axis=-1, keepdims=True) + EPS)
    o = o.reshape(B, T, D_HGRN) * out_norm.astype(jnp.float32) * jax.nn.silu(zg.astype(jnp.float32))
    pool_out, new_hist = pool_mixer(pool_hist.astype(zp.dtype), zp, n_hist, pool_w, pool_scale)
    mix = jnp.concatenate([o.astype(h.dtype), pool_out.astype(h.dtype)], axis=-1) @ w_out
    h = h + mix
    h = h + peer_ffn(rmsnorm(h, norm_ffn), peer_w_query, peer_subkeys, peer_u, peer_v)
    return h, S_new.astype(h.dtype), new_hist

def setup_inputs(seed: int = 0) -> dict:
    key = jax.random.key(seed)
    ks = jax.random.split(key, 18)
    f32 = jnp.float32

    def nrm(k, shape, scale):
        return jax.random.normal(k, shape, f32) * scale

    return {
        'x_prompt': nrm(ks[0], (BATCH, SEQ, D_MODEL), 1.0),
        'x_sample': nrm(ks[1], (DEC_BATCH, DEC_SEQ, D_MODEL), 1.0),
        'state_hgrn': nrm(ks[2], (DEPTH, DEC_BATCH, H_A, DK, DV), 0.5),
        'cache_pool': nrm(ks[3], (DEPTH, DEC_BATCH, POOL_HIST, D_POOL), 1.0),
        'meta_tokens': nrm(ks[4], (N_META, D_MODEL), 1.0),
        'norm_mix': 1.0 + nrm(ks[5], (DEPTH, D_MODEL), 0.02),
        'w_in': nrm(ks[6], (DEPTH, D_MODEL, D_IN_PROJ), D_MODEL ** -0.5),
        'hgrn_lb_logits': nrm(ks[7], (DEPTH + 1, D_HGRN), 0.5),
        'hgrn_out_norm': 1.0 + nrm(ks[8], (DEPTH, D_HGRN), 0.02),
        'pool_w': nrm(ks[9], (DEPTH, N_POOL_GROUPS, POOL_GW, POOL_GW), POOL_GW ** -0.5),
        'pool_scale': 0.5 + nrm(ks[10], (DEPTH, D_POOL), 0.05),
        'w_out': nrm(ks[11], (DEPTH, D_MIX, D_MODEL), D_MIX ** -0.5),
        'norm_ffn': 1.0 + nrm(ks[12], (DEPTH, D_MODEL), 0.02),
        'peer_w_query': nrm(ks[13], (DEPTH, D_MODEL, PEER_HEADS * PEER_DKEY), D_MODEL ** -0.5),
        'peer_subkeys': nrm(ks[14], (DEPTH, PEER_HEADS, 2, N_KEYS, PEER_DKEY // 2), (PEER_DKEY // 2) ** -0.5),
        'peer_u': nrm(ks[15], (DEPTH, N_EXPERTS, D_MODEL), D_MODEL ** -0.5),
        'peer_v': nrm(ks[16], (DEPTH, N_EXPERTS, D_MODEL), PEER_HEADS ** -0.5),
        'norm_final': 1.0 + nrm(ks[17], (D_MODEL,), 0.02),
    }

def reference(x_prompt, x_sample, state_hgrn, cache_pool, meta_tokens, norm_mix, w_in,
              hgrn_lb_logits, hgrn_out_norm, pool_w, pool_scale, w_out, norm_ffn,
              peer_w_query, peer_subkeys, peer_u, peer_v, norm_final):
    lb_all = jnp.cumsum(jax.nn.softmax(hgrn_lb_logits.astype(jnp.float32), axis=0), axis=0)
    Bp = x_prompt.shape[0]
    meta = jnp.broadcast_to(meta_tokens[None].astype(x_prompt.dtype), (Bp, N_META, D_MODEL))
    hp = jnp.concatenate([meta, x_prompt], axis=1)
    hs = x_sample
    S_p0 = jnp.zeros((Bp, H_A, DK, DV), jnp.float32)
    pool_p0 = jnp.zeros((Bp, POOL_HIST, D_POOL), x_prompt.dtype)
    sp_list, cp_list, ss_list, cs_list = [], [], [], []
    for l in range(DEPTH):
        w = (lb_all[l], norm_mix[l], w_in[l], hgrn_out_norm[l], pool_w[l], pool_scale[l],
             w_out[l], norm_ffn[l], peer_w_query[l], peer_subkeys[l], peer_u[l], peer_v[l])
        hp, sp, cp = trunk_layer(hp, S_p0, pool_p0, 0, *w)
        hs, ss, cs = trunk_layer(hs, state_hgrn[l], cache_pool[l], POOL_HIST, *w)
        sp_list.append(sp)
        cp_list.append(cp)
        ss_list.append(ss)
        cs_list.append(cs)
    y_prompt = rmsnorm(hp[:, N_META:], norm_final)
    y_sample = rmsnorm(hs, norm_final)
    state_hgrn_prompt = jnp.stack(sp_list, axis=0)
    cache_pool_prompt = jnp.stack(cp_list, axis=0)
    state_hgrn_sample = jnp.stack(ss_list, axis=0)
    cache_pool_sample = jnp.stack(cs_list, axis=0)
    return (y_prompt, y_sample, state_hgrn_prompt, cache_pool_prompt, state_hgrn_sample, cache_pool_sample)


_drawn_inputs = setup_inputs


def setup_inputs(seed=0):
    import zlib

    import numpy as np

    out = dict(_drawn_inputs(seed))
    spreads = {}
    factors = {'hgrn_out_norm': 9.694,
     'norm_final': 23.333,
     'norm_ffn': 11.181,
     'cache_pool': 4.809,
     'pool_scale': 4.802}
    for name, (base, spread) in spreads.items():
        noise = np.random.default_rng([zlib.crc32(name.encode()), seed]).standard_normal(out[name].shape)
        drawn = base * np.exp(spread * noise) if base else spread * noise
        out[name] = __import__('jax').numpy.asarray(drawn.astype(out[name].dtype))
    for name, factor in factors.items():
        out[name] = (out[name] * factor).astype(out[name].dtype)
    return out
```

```python
import concourse.bass as bass
from concourse import mybir
from contextlib import ExitStack

FP32 = mybir.dt.float32
BF16 = mybir.dt.bfloat16
U32 = mybir.dt.uint32
ALU = mybir.AluOpType
ACT = mybir.ActivationFunctionType
AX_X = mybir.AxisListType.X

P = 128
D = 1024
DC = D // P
SEQ, META, SAMP = 512, 16, 32
H_A = 4
HIST = 15
WINDOWS = (2, 4, 8, 16)
PEER_H, TOPK, NKEYS = 8, 16, 128
EPS = 1e-6
NEG = -3.0e38

GAP = 16
N = (META + P + GAP + SAMP, SEQ - P)
COLS = sum(N)
SAMP0 = META + P + GAP
NMAX = max(N)
PAD = 16
ZW = NMAX + PAD
CHUNKS = [(0, 0, META, 0, "p"), (0, META, P, 7, "p"), (0, SAMP0, SAMP, 5, "s"),
          (1, 0, P, 7, "p"), (1, P, P, 7, "p"), (1, 2 * P, P, 7, "p")]

B_IN, B_OUT, B_Q = 20, 8, 16
B_ALL = B_IN + B_OUT + B_Q
WSLOTS = 4
WQ = D + NKEYS

TILES = [("t0", 0, 8), ("pk", 8, 2), ("t1", 10, 8), ("t2", 18, 8), ("t3", 26, 8)]
STEPS = 34
G0_STEPS = 10
RU, RV, RD = 8, 4, 4


def count_before(per_chunk, chunk):
    return sum(per_chunk(c) for c in CHUNKS[:chunk])


def build(nc, xT, w_io, w_q, pool_w, vecs, masks, ident_d, sel_d, small_d, cacheT, state_d, nf_d, peer_u, peer_v,
          y_prompt, y_sample, sp_out, ss_out, cp_out, cs_out):
    ctx = ExitStack()
    with ctx:
        def sb(name, shape, dt=FP32):
            return ctx.enter_context(nc.sbuf_tensor(name, shape, dt))

        def sem(name):
            return ctx.enter_context(nc.semaphore(name))

        hT = sb("hT", [P, DC, NMAX])
        mix = sb("mix", [P, DC, NMAX])
        S_FLOATS = G0_STEPS * 2 * NKEYS
        arena = sb("arena", [P, S_FLOATS + 20 * ZW])
        lev = sb("lev", [P, 7 * 4 * P])
        wring = sb("wring", [P, WSLOTS, WQ])
        mask = sb("mask", [P, 8, P])
        nf = sb("nf", [P, D])
        ident = sb("ident", [P, P])
        sel = sb("sel", [P, SAMP])
        ones = sb("ones", [P, P])
        small = sb("small", [P, 16 + 4 * 16])
        pw = sb("pw", [P, 4, P])
        vec = sb("vec", [P, 40])
        lbt = sb("lbt", [P, 12])
        epst = sb("epst", [P, 1])
        cache = sb("cache", [P, 4, HIST])
        carry = sb("carry", [P, 4, HIST])
        cs_buf = sb("cs_buf", [P, 4, HIST])
        cp_buf = sb("cp_buf", [P, 4, HIST])
        Sp = sb("Sp", [P, 4, P])
        Ss = sb("Ss", [P, 4, P])
        htok0 = sb("htok0", [P, D])
        htoks = sb("htoks", [SAMP, D])
        xtok0 = sb("xtok0", [P, D])
        xtokp = sb("xtokp", [P, D])
        Ur = sb("Ur", [P, RU, D])
        Vr = sb("Vr", [P, RV, D])
        ctmp = sb("ctmp", [P, 2 * 8 * P + 2 * P + 4 * 4 * P])
        dec = sb("dec", [P, 4])
        stg = sb("stg", [P, 2, 2, NKEYS])
        rest = sb("rest", [P, 2, NKEYS])
        cand = sb("cand", [P, TOPK * TOPK])
        onehot = sb("onehot", [P, 2, TOPK, TOPK])
        sv = sb("sv", [P, 2, TOPK])
        si = sb("si", [P, 2, TOPK], U32)
        top = sb("top", [P, 2, TOPK])
        pos = sb("pos", [P, TOPK], U32)
        hilo = sb("hilo", [P, 2, TOPK], U32)
        ab = sb("ab", [P, 2, TOPK])
        idxU = sb("idxU", [P, 2, TOPK], U32)
        idxV = sb("idxV", [P, 2, TOPK], U32)
        ex = sb("ex", [P, 2, TOPK])
        exs = sb("exs", [P, 2, 4])
        adot = sb("adot", [P, 2, TOPK])
        ge = sb("ge", [P, 2, TOPK])
        wgt = sb("wgt", [P, 2, TOPK])
        diag = sb("diag", [P, RD, P])
        ydump = sb("ydump", [P, D], BF16)
        yst = sb("yst", [P, 4])
        zb = sb("zb", [1, 512], BF16)

        nw = (vec[:, 0:8], vec[:, 8:16])
        onorm, pscale, lg = vec[:, 16:20], vec[:, 20:24], vec[:, 24:32]
        lb, oml = lbt[:, 0:4], lbt[:, 4:8]
        iota16, rcnt = small[:, 0:16], small[:, 16:80].rearrange("p (g t) -> p g t", g=4)
        zf_ = arena[:, S_FLOATS:S_FLOATS + 20 * ZW]
        z = zf_.rearrange("p (s h c) -> p s h c", s=5, h=4)
        SQ, SF, SI, SG, SP_ = range(5)
        bufs = [lev[:, 0:4 * ZW].rearrange("p (g c) -> p g c", g=4),
                lev[:, 4 * ZW:8 * ZW].rearrange("p (g c) -> p g c", g=4)]
        xn2 = lev[:, 0:DC * NMAX].rearrange("p (c n) -> p c n", c=DC)
        msk = [ctmp[:, i * 1024:(i + 1) * 1024] for i in range(2)]
        AT = [ctmp[:, 2048 + i * P:2048 + (i + 1) * P] for i in range(2)]
        o4 = 2048 + 2 * P
        eb, ek, vtok, ktok = [ctmp[:, o4 + i * 512:o4 + (i + 1) * 512] for i in range(4)]
        osq, ors = [msk[0][:, i * 512:(i + 1) * 512] for i in range(2)]
        sqb = [ctmp[:, i * NMAX:(i + 1) * NMAX] for i in range(2)]
        rst = ctmp[:, 2 * NMAX:3 * NMAX]
        qT = [ctmp[:, (3 + i) * NMAX:(4 + i) * NMAX] for i in range(2)]
        htok = {"t0": htok0[:], "pk": htoks[:]}
        xtok = {"t0": xtok0[:], "pk": xtokp[:]}
        mixf, hTf = mix[:].rearrange("p c n -> p (c n)"), hT[:].rearrange("p c n -> p (c n)")
        for i in range(3):
            htok[f"t{i + 1}"] = mixf[:, i * D:(i + 1) * D]
            xtok[f"t{i + 1}"] = hTf[:, i * D:(i + 1) * D]

        P01 = ctx.enter_context(nc.psum_tensor("P01", [P, 1024], FP32))
        P23 = ctx.enter_context(nc.psum_tensor("P23", [P, 1024], FP32))
        b4, b5, b6, b7 = [ctx.enter_context(nc.psum_tensor(f"b{i}", [P, 512], FP32)) for i in (4, 5, 6, 7)]
        TB = (b4, b5)

        x_in = [sem(f"x_in{g}") for g in range(2)]
        const_in, const_set = sem("const_in"), sem("const_set")
        w_in = [sem(f"w_in{r}") for r in range(WSLOTS)]
        blocks_done = sem("blocks_done")
        lb_diff, lb_set = sem("lb_diff"), sem("lb_set")
        sq_done = [[sem(f"sq_done{g}{k}") for k in range(2)] for g in range(2)]
        ss_done = [[sem(f"ss_done{g}{k}") for k in range(2)] for g in range(2)]
        xn_done = [[sem(f"xn_done{g}{k}") for k in range(2)] for g in range(2)]
        z_free = [sem(f"z_free{g}") for g in range(2)]
        h_free = [sem(f"h_free{g}") for g in range(2)]
        q_free = [sem(f"q_free{g}") for g in range(2)]
        pool_step = [sem(f"pool_step{g}") for g in range(2)]
        pool_mm = [sem(f"pool_mm{g}") for g in range(2)]
        pool_out = [sem(f"pool_out{g}") for g in range(2)]
        act_prep = [sem(f"act_prep{g}") for g in range(2)]
        dve_prep = [sem(f"dve_prep{g}") for g in range(2)]
        lsub, lexp, lmul, ctr, ctr_out, lmm, at_done, o_mm, s_mm, s_done, on_done, osum_done, mo_done = [
            sem(n) for n in ("lsub", "lexp", "lmul", "ctr", "ctr_out", "lmm", "at_done", "o_mm", "s_mm", "s_done",
                             "on_done", "osum_done", "mo_done")]
        tr_mm = [sem(f"tr_mm{g}") for g in range(2)]
        tr_out = [sem(f"tr_out{g}") for g in range(2)]
        sc_mm = [sem(f"sc_mm{g}") for g in range(2)]
        sc_free = [sem(f"sc_free{g}") for g in range(2)]
        staged, topk, exp_done, gelu_done, w_done, diag_done = [sem(n) for n in (
            "staged", "topk", "exp_done", "gelu_done", "w_done", "diag_done")]
        idx_copied = sem("idx_copied")
        u_free, v_free = sem("u_free"), sem("v_free")
        u_in = [sem(f"u_in{r}") for r in range(RU)]
        v_in = [sem(f"v_in{r}") for r in range(RV)]
        acc_open, acc_close, y_sum, y_rstd, y_done, stored = [sem(n) for n in (
            "acc_open", "acc_close", "y_sum", "y_rstd", "y_done", "stored")]

        full = lambda c: 1 if c[3] else 0
        n_lsub = lambda c: 2 * c[3]
        n_lexp = lambda c: 5 + full(c) + c[3]
        n_lmul = lambda c: 1 + full(c) + 2 * c[3]
        n_ctr = lambda c: 2
        n_lmm = lambda c: 4 * full(c)
        n_at = lambda c: 8 * full(c)
        n_smm = lambda c: 1
        n_sd = lambda c: 1 if not full(c) else 4
        n_on = lambda c: 3 * full(c)
        n_os = lambda c: full(c)
        n_mo = lambda c: 2 * full(c)
        PL = ((16, 10))
        DP_K, DP_G = 5, 9
        n_scans = lambda g: 4 * sum(1 for c in CHUNKS if c[0] == g)
        group_tiles = ((("t0", META), ("pk", SAMP0)), (("t1", 0), ("t2", P), ("t3", 2 * P)))
        n_tr = (8, 12)
        TK = 22

        waited = {n: sem(f"waited_{n}") for n in ("vector", "gpsimd")}

        def own(eng):
            eng.sem_inc(waited["gpsimd" if eng is nc.gpsimd else "vector"], 1)

        plan = []
        for g in range(2):
            plan += [("norm", g, 0), ("proj", g), ("prep", g)]
            plan += [("chunk", c) for c in range(len(CHUNKS)) if CHUNKS[c][0] == g]
            plan += [("w_out", g), ("norm", g, 1), ("tok", g), ("query", g)]
            first, last = (0, G0_STEPS) if g == 0 else (G0_STEPS, STEPS)
            plan += [("first", first)]
            ends = {t[1] + t[2]: i for i, t in enumerate(TILES)}
            s = first
            while s < last:
                in_tile = [t for t in TILES if t[1] <= s < t[1] + t[2]][0]
                plan.append(("step", s, True, s > first, s + 1 < last))
                if s in ends and s > first:
                    plan.append(("y_sum", ends[s]))
                if s - 1 in ends and s - 1 > first:
                    plan.append(("y_out", ends[s - 1]))
                s += 1
                if s == in_tile[1] + 2 and in_tile[2] == 8:
                    pairs = 2 if in_tile[1] + 8 == last else 3
                    plan.append(("loop", s, pairs))
                    s += 2 * pairs
            plan.append(("step", last, False, True, False))
            plan += [("y_sum", ends[last]), ("y_out", ends[last])]

        def tile_of(s):
            return [i for i, t in enumerate(TILES) if t[1] <= s < t[1] + t[2]][0]

        def run(eng, parts):
            for kind, *a in plan:
                if kind == "loop":
                    s0, pairs = a
                    with eng.Fori(0, pairs) as k:
                        for par in range(2):
                            parts["step"](k * 2 + (s0 + par), s0 + par, True, True, True)
                elif kind in parts:
                    if kind == "step":
                        parts["step"](a[0], *a)
                    else:
                        parts[kind](*a)

        block = ctx.enter_context(nc.Block())

        def ysteps(sp, a, b):
            for i in range(a, b):
                name = TILES[i][0]
                sp.wait_ge(y_done, i + 1)
                if name == "pk":
                    sp.dma_start(y_sample, htok[name]).then_inc(stored, 16)
                else:
                    n = int(name[1])
                    sp.dma_start(y_prompt[n * P:(n + 1) * P, :], htok[name]).then_inc(stored, 16)

        @block.sync
        def _(sp):
            sp.dma_start(hT[:, :, 0:N[0]], xT[:, :, 0:N[0]]).then_inc(x_in[0], 16)
            for dst, src in ((vec[:, 0:32], vecs), (small[:], small_d), (ident[:], ident_d), (pw[:], pool_w),
                             (mask[:], masks), (cache[:], cacheT), (Ss[:], state_d), (sel[:], sel_d),
                             (nf[:], nf_d.partition_broadcast(P))):
                sp.dma_start(dst, src).then_inc(const_in, 16)

            def load(B, r, query):
                if query:
                    sp.dma_start(wring[:, r, :], w_q[bass.ds(B, 1), :, :].rearrange("b p m -> p (b m)")
                                 ).then_inc(w_in[r], 16)
                else:
                    sp.dma_start(wring[:, r, 0:D], w_io[bass.ds(B, 1), :, :].rearrange("b p m -> p (b m)")
                                 ).then_inc(w_in[r], 16)

            for g in range(2):
                base = g * B_ALL
                if g:
                    sp.wait_ge(tr_out[0], n_tr[0])
                    sp.wait_ge(xn_done[0][1], DC)
                    sp.dma_start(hT[:, :, 0:N[1]], xT[:, :, N[0]:COLS]).then_inc(x_in[1], 16)
                for r in range(WSLOTS):
                    if g:
                        sp.wait_ge(blocks_done, base + r - 1)
                    load(r, r, False)
                with sp.Fori(1, (B_IN + B_OUT) // WSLOTS) as k:
                    for r in range(WSLOTS):
                        sp.wait_ge(blocks_done, k * WSLOTS + (base + r + 1 - WSLOTS))
                        load(k * WSLOTS + r, r, False)
                for r in range(WSLOTS):
                    sp.wait_ge(blocks_done, base + B_IN + B_OUT + r + 1 - WSLOTS)
                    load(r, r, True)
                with sp.Fori(1, B_Q // WSLOTS) as k:
                    for r in range(WSLOTS):
                        sp.wait_ge(blocks_done, k * WSLOTS + (base + B_IN + B_OUT + r - 1))
                        load(k * WSLOTS + r, r, True)
            sp.wait_ge(pool_step[1], 2)
            sp.dma_start(cs_out, cs_buf[:]).then_inc(stored, 16)
            sp.dma_start(cp_out, cp_buf[:]).then_inc(stored, 16)
            sp.wait_ge(s_done, count_before(n_sd, 6))
            sp.dma_start(ss_out, Ss[:]).then_inc(stored, 16)
            sp.dma_start(sp_out, Sp[:]).then_inc(stored, 16)
            ysteps(sp, 0, 5)
            sp.wait_ge(stored, 16 * 9)

        @block.gpsimd
        def _(pool):
            nc.gpsimd.memset(ones[:], 1.0).then_inc(const_set, 1)
            nc.gpsimd.memset(epst[:], EPS).then_inc(const_set, 1)
            nc.gpsimd.memset(zb[:], 0.0).then_inc(const_set, 1)

            def step(s, s0, do_u, do_v, _next):
                par = s0 % 2
                if do_u:
                    pool.wait_ge(topk, s * TK + TK)
                    own(pool)
                for j in range(TOPK):
                    if do_u:
                        pool.wait_ge(u_free, s * TOPK + j + 1)
                        own(pool)
                        pool.indirect_dma_start(Ur[:, j % RU, :], None, peer_u, bass.IndirectOffsetOnAxis(
                            ap=idxU[:, par, j:j + 1], axis=0)).then_inc(u_in[j % RU], 16)
                    if do_v:
                        if j == 0:
                            pool.wait_ge(idx_copied, s)
                        pool.wait_ge(v_free, (s - 1) * TOPK + j + 1)
                        own(pool)
                        pool.indirect_dma_start(Vr[:, j % RV, :], None, peer_v, bass.IndirectOffsetOnAxis(
                            ap=idxV[:, 1 - par, j:j + 1], axis=0)).then_inc(v_in[j % RV], 16)
                if do_u:
                    nc.gpsimd.tensor_copy(idxV[:, par, :], idxU[:, par, :]).then_inc(idx_copied, 1)

            run(pool, {"step": step})

        @block.scalar
        def _(act):
            A = nc.scalar.activation

            def norm(g, k):
                n = N[g]
                if k == 0:
                    act.wait_ge(x_in[g], 16)
                    act.wait_ge(const_set, 2)
                else:
                    act.wait_ge(h_free[g], 2 + DC)
                for c in range(DC):
                    if c >= 2:
                        act.wait_ge(ss_done[g][k], c - 1)
                    A(sqb[c % 2][:, 0:n], hT[:, c, 0:n], ACT.Square).then_inc(sq_done[g][k], 1)
                act.wait_ge(ss_done[g][k], DC)
                A(rst[:, 0:n], P23[:, 512:512 + n], ACT.Ln, scale=1.0 / D, bias=epst[:]).then_inc(sq_done[g][k], 1)
                act.wait_ge(sq_done[g][k], DC + 1)
                A(rst[:, 0:n], rst[:, 0:n], ACT.Exp, scale=-0.5).then_inc(sq_done[g][k], 1)

            def proj(g):
                n = N[g]
                act.sem_inc(z_free[g], 2)
                with act.Fori(0, B_IN // WSLOTS) as k:
                    for r in range(WSLOTS):
                        act.wait_ge(blocks_done, k * WSLOTS + (g * B_ALL + r + 1))
                        A(zf_[:, bass.ds(k * (WSLOTS * ZW) + (r * ZW + PAD), n)], P01[:, r % 2 * 512:r % 2 * 512 + n],
                          ACT.Copy).then_inc(z_free[g], 1)

            def prep(g):
                n, w = N[g], slice(PAD, PAD + N[g])
                tA = lev[:, 0:4 * n].rearrange("p (h c) -> p h c", h=4)
                tB = lev[:, 4 * n:8 * n].rearrange("p (h c) -> p h c", h=4)
                tC = mix[:, 0:4, 0:n]
                if g == 0:
                    act.wait_ge(lb_diff, 1)
                    A(lb, lbt[:, 8:12], ACT.Sigmoid).then_inc(lb_set, 1)
                    A(oml, lbt[:, 8:12], ACT.Sigmoid, scale=-1.0).then_inc(lb_set, 1)
                for i in range(4):
                    act.wait_ge(pool_mm[g], i + 1)
                    A(mix[:, 4 + i, 0:n], P23[:, i % 2 * 512:i % 2 * 512 + n], ACT.Copy,
                      scale=pscale[:, i:i + 1]).then_inc(pool_out[g], 1)
                A(tC, z[:, SQ, :, w], ACT.Sigmoid).then_inc(act_prep[g], 1)
                A(tA, z[:, SF, :, w], ACT.Sigmoid).then_inc(act_prep[g], 1)
                A(tB, z[:, SF, :, w], ACT.Sigmoid, scale=-1.0).then_inc(act_prep[g], 1)
                act.wait_ge(dve_prep[g], DP_K)
                A(tB, z[:, SG, :, w], ACT.Sigmoid).then_inc(act_prep[g], 1)
                act.wait_ge(act_prep[g], 2)
                act.wait_ge(lb_set, 2)
                for h in range(4):
                    A(tA[:, h, :], tA[:, h, :], ACT.Ln, scale=oml[:, h:h + 1], bias=lb[:, h:h + 1]).then_inc(act_prep[g], 1)

            def chunk(ci):
                g, c0, T, nl, _ = c = CHUNKS[ci]
                b = z[:, SF, :, PAD + c0:PAD + c0 + T]
                last = b[:, :, T - 1]
                v4 = lambda t: t[:, 0:4 * T].rearrange("p (h t) -> p h t", h=4)
                scans = DP_G + 4 * (1 + sum(1 for x in CHUNKS[:ci] if x[0] == g))
                if ci:
                    act.wait_ge(s_mm, count_before(n_smm, ci))
                act.wait_ge(ctr, count_before(n_ctr, ci) + 1)
                A(vtok[0:T, :], b4[0:T, :], ACT.Copy).then_inc(ctr_out, 1)
                act.wait_ge(dve_prep[g], scans)
                if nl:
                    A(v4(eb), b, ACT.Exp).then_inc(lexp, 1)
                for h in range(4):
                    A(ek[:, h * T:(h + 1) * T], b[:, h, :], ACT.Exp, scale=-1.0, bias=last[:, h:h + 1]).then_inc(lexp, 1)
                A(dec[:], last, ACT.Exp).then_inc(lexp, 1)
                for l in range(nl):
                    act.wait_ge(lsub, count_before(n_lsub, ci) + 2 * l + 2)
                    lv = lev[:, l * 4 * T:(l + 1) * 4 * T]
                    A(lv, lv, ACT.Exp).then_inc(lexp, 1)
                act.wait_ge(ctr, count_before(n_ctr, ci) + 2)
                A(ktok[0:T, :], b5[0:T, :], ACT.Copy).then_inc(ctr_out, 1)
                if nl:
                    act.wait_ge(o_mm, count_before(n_lmm, ci) + 4)
                    A(osq[:, 0:4 * T], b4[:, 0:4 * T], ACT.Square).then_inc(on_done, 1)
                    act.wait_ge(osum_done, count_before(n_os, ci) + 1)
                    A(ors[:, 0:4 * T], P23[:, 0:4 * T], ACT.Ln, scale=1.0 / P, bias=epst[:]).then_inc(on_done, 1)
                    act.wait_ge(on_done, count_before(n_on, ci) + 2)
                    A(ors[:, 0:4 * T], ors[:, 0:4 * T], ACT.Exp, scale=-0.5).then_inc(on_done, 1)

            def tok(g):
                u = 0
                for src in (htok, xtok):
                    for name, _ in group_tiles[g]:
                        rows = SAMP if (name == "pk" and src is htok) else P
                        for half in range(2):
                            act.wait_ge(tr_mm[g], u + 1)
                            A(src[name][0:rows, half * 512:(half + 1) * 512], TB[u % 2][0:rows, :],
                              ACT.Copy).then_inc(tr_out[g], 1)
                            u += 1

            def query(g):
                n = N[g]
                act.sem_inc(q_free[g], 2)
                act.sem_inc(sc_free[g], 2)
                with act.Fori(0, B_Q // WSLOTS) as k:
                    def q_copy(r):
                        act.wait_ge(blocks_done, k * WSLOTS + (g * B_ALL + B_IN + B_OUT + r + 1))
                        A(qT[r % 2][:, 0:n], P01[:, r % 2 * 512:r % 2 * 512 + n], ACT.Copy).then_inc(q_free[g], 1)

                    def s_copy(r):
                        act.wait_ge(sc_mm[g], k * WSLOTS + (r + 1))
                        o = r % 2 * 512
                        if g:
                            dst = arena[:, S_FLOATS:S_FLOATS + 3 * 2048].rearrange("p (t s) -> p t s", t=3)
                            A(dst[:, :, bass.ds(k * NKEYS + r * 512, NKEYS)],
                              P23[:, o:o + 384].rearrange("p (t s) -> p t s", t=3), ACT.Copy).then_inc(sc_free[g], 1)
                        else:
                            A(arena[:, bass.ds(k * NKEYS + r * 512, NKEYS)], P23[:, o:o + P], ACT.Copy)
                            q = slice(SAMP * r, SAMP * (r + 1))
                            A(arena[q, bass.ds(k * NKEYS + 8 * 256, NKEYS)], P23[q, o + P:o + 2 * P],
                              ACT.Copy).then_inc(sc_free[g], 1)

                    q_copy(0)
                    q_copy(1)
                    s_copy(0)
                    q_copy(2)
                    s_copy(1)
                    q_copy(3)
                    s_copy(2)
                    s_copy(3)

            def stage(s, s0):
                if s0 >= 2:
                    act.wait_ge(topk, (s - 1) * TK)
                A(stg[:, s0 % 2].rearrange("p a n -> p (a n)"), arena[:, bass.ds(s * 256, 256)], ACT.Copy).then_inc(staged, 1)

            def exps(s, s0):
                par = s0 % 2
                act.wait_ge(topk, s * TK + 16)
                if s0 >= 2:
                    act.wait_ge(w_done, (s - 1) * 2)
                A(exs[:, par, 0:1], top[:, par, 0:1], ACT.Copy, scale=-1.0).then_inc(exp_done, 1)
                act.wait_ge(exp_done, s * 2 + 1)
                A(ex[:, par, :], top[:, par, :], ACT.Exp, bias=exs[:, par, 0:1],
                  accum_out=exs[:, par, 1:2]).then_inc(exp_done, 1)

            def first(s):
                if s:
                    act.wait_ge(sc_free[1], 2 + B_Q)
                else:
                    act.wait_ge(sc_free[0], 2 + B_Q)
                stage(s, s)
                exps(s, s)

            def step(s, s0, do_u, do_v, nxt):
                if nxt:
                    stage(s + 1, s0 + 1)
                if do_v:
                    par = 1 - s0 % 2
                    act.wait_ge(u_free, s * TOPK + RU)
                    A(ge[:, par, :], adot[:, par, :], ACT.Gelu).then_inc(gelu_done, 1)
                    t = TILES[tile_of(s0 - 1)][0]
                    for j in range(TOPK):
                        if j == 0:
                            act.wait_ge(w_done, s * 2)
                        act.wait_ge(v_free, (s - 1) * TOPK + (j + 1 + RV - RD))
                        if t == "pk":
                            A(diag[:, j % RD, 0:SAMP], sel[:], ACT.Copy, scale=wgt[:, par, j:j + 1]).then_inc(diag_done, 1)
                        else:
                            A(diag[:, j % RD, :], ident[:], ACT.Copy, scale=wgt[:, par, j:j + 1]).then_inc(diag_done, 1)
                if nxt:
                    exps(s + 1, s0 + 1)

            def y_sum_(i):
                name = TILES[i][0]
                rows = SAMP if name == "pk" else P
                act.wait_ge(y_sum, 2 * (i + 1))
                A(ydump[0:rows, :], htok[name][0:rows, :], ACT.Square, accum_out=yst[0:rows, 0:1]).then_inc(y_rstd, 1)
                act.wait_ge(y_rstd, 3 * i + 1)
                A(yst[0:rows, 1:2], yst[0:rows, 0:1], ACT.Ln, scale=1.0 / D, bias=epst[0:rows, :]).then_inc(y_rstd, 1)
                act.wait_ge(y_rstd, 3 * i + 2)
                A(yst[0:rows, 2:3], yst[0:rows, 1:2], ACT.Exp, scale=-0.5).then_inc(y_rstd, 1)

            act.wait_ge(const_in, 16 * 9)
            run(act, {"norm": norm, "proj": proj, "prep": prep, "chunk": chunk, "tok": tok, "query": query,
                      "first": first, "step": step, "y_sum": y_sum_})

        @block.vector
        def _(dve):
            V = nc.vector

            def norm(g, k):
                n = N[g]
                dve.wait_ge(sq_done[g][k], DC + 2)
                dst = xn2 if k else mix
                for c in range(DC):
                    V.scalar_tensor_tensor(out=dst[:, c, 0:n], in0=hT[:, c, 0:n], scalar=nw[k][:, c:c + 1],
                                           in1=rst[:, 0:n], op0=ALU.mult, op1=ALU.mult).then_inc(xn_done[g][k], 1)

            def prep(g):
                n, L, w = N[g], PAD + N[g], slice(PAD, PAD + N[g])
                u = z[:, SP_]
                ps, cnt = pool_step[g], [0]

                def did(ins, wait=True):
                    ins.then_inc(ps, 1)
                    cnt[0] += 1
                    if wait:
                        dve.wait_ge(ps, cnt[0])

                if g == 0:
                    V.tensor_tensor(lbt[:, 8:12], lg[:, 0:4], lg[:, 4:8], ALU.subtract).then_inc(lb_diff, 1)
                dve.wait_ge(z_free[g], 2 + B_IN)
                if g == 0:
                    did(V.memset(u[:, :, 1:PAD], 0.0), False)
                    did(V.tensor_copy(u[:, :, PAD + SAMP0 - HIST:PAD + SAMP0], cache[:]), False)
                    did(V.tensor_copy(carry[:], u[:, :, PAD + META + P - HIST:PAD + META + P]), False)
                    did(V.tensor_copy(cs_buf[:], u[:, :, L - HIST:L]))
                else:
                    did(V.tensor_copy(u[:, :, 1:PAD], carry[:]), False)
                    did(V.tensor_copy(cp_buf[:], u[:, :, L - HIST:L]))
                a, b = bufs
                did(V.tensor_tensor(a[:, :, 2:L], u[:, :, 2:L], u[:, :, 1:L - 1], ALU.add))
                did(V.tensor_tensor(b[:, 1:4, 4:L], a[:, 1:4, 4:L], a[:, 1:4, 2:L - 2], ALU.add))
                did(V.tensor_tensor(a[:, 2:4, 8:L], b[:, 2:4, 8:L], b[:, 2:4, 4:L - 4], ALU.add))
                did(V.tensor_tensor(b[:, 3, 16:L], a[:, 3, 16:L], a[:, 3, 8:L - 8], ALU.add))
                if g == 0:
                    for i in range(4):
                        t = bufs[i % 2][:, i, PAD:PAD + META]
                        did(V.tensor_tensor(t, t, rcnt[:, i, :], ALU.mult), i == 3)
                for i in range(4):
                    t = bufs[i % 2][:, i, w]
                    did(V.scalar_tensor_tensor(out=t, in0=t, scalar=1.0 / WINDOWS[i], in1=u[:, i, w],
                                               op0=ALU.mult, op1=ALU.subtract), False)
                assert cnt[0] == PL[g]
                dp = dve_prep[g]
                tA = lev[:, 0:4 * n].rearrange("p (h c) -> p h c", h=4)
                tB = lev[:, 4 * n:8 * n].rearrange("p (h c) -> p h c", h=4)
                tC = mix[:, 0:4, 0:n]
                dve.wait_ge(ps, PL[g])
                dve.wait_ge(act_prep[g], 1)
                V.scalar_tensor_tensor(out=z[:, SQ, :, w], in0=z[:, SQ, :, w], scalar=float(P) ** -0.5, in1=tC,
                                       op0=ALU.mult, op1=ALU.mult).then_inc(dp, 1)
                dve.wait_ge(act_prep[g], 3)
                dve.wait_ge(lb_set, 2)
                for h in range(4):
                    V.tensor_scalar(z[:, SP_, h, w], tB[:, h, :], oml[:, h:h + 1], None, ALU.mult).then_inc(dp, 1)
                dve.wait_ge(act_prep[g], 4)
                for h in range(4):
                    V.scalar_tensor_tensor(out=z[:, SG, h, w], in0=tB[:, h, :], scalar=onorm[:, h:h + 1],
                                           in1=z[:, SG, h, w], op0=ALU.mult, op1=ALU.mult).then_inc(dp, 1)
                dve.wait_ge(act_prep[g], 8)
                for _, c0, T, _, _ in [c for c in CHUNKS if c[0] == g]:
                    for h in range(4):
                        V.tensor_tensor_scan(out=z[:, SF, h, PAD + c0:PAD + c0 + T], data0=ones[:, 0:T],
                                             data1=tA[:, h, c0:c0 + T], initial=0.0, op0=ALU.mult,
                                             op1=ALU.add).then_inc(dp, 1)

            def chunk(ci):
                g, c0, T, nl, stream = CHUNKS[ci]
                cs = slice(PAD + c0, PAD + c0 + T)
                q, b, k_, G = z[:, SQ, :, cs], z[:, SF, :, cs], z[:, SP_, :, cs], z[:, SG, :, cs]
                v4 = lambda t: t[:, 0:4 * T].rearrange("p (h t) -> p h t", h=4)
                S = Sp if stream == "p" else Ss
                le, lm, at = (count_before(x, ci) for x in (n_lexp, n_lmul, n_at))
                scans = DP_G + n_scans(g)
                dve.wait_ge(dve_prep[g], scans)

                def halves(l):
                    hw = 1 << l
                    f = lambda x: x.rearrange("p h (n two w) -> p h n two w", two=2, w=hw)
                    lv = f(v4(lev[:, l * 4 * T:(l + 1) * 4 * T]))
                    ref = f(b)[:, :, :, 0, hw - 1:hw].broadcast_to([P, 4, T // (2 * hw), hw])
                    return f, lv, ref

                for l in range(nl):
                    f, lv, ref = halves(l)
                    V.tensor_tensor(lv[:, :, :, 1, :], f(b)[:, :, :, 1, :], ref, ALU.subtract).then_inc(lsub, 1)
                    V.tensor_tensor(lv[:, :, :, 0, :], ref, f(b)[:, :, :, 0, :], ALU.subtract).then_inc(lsub, 1)
                if nl:
                    dve.wait_ge(lexp, le + 1)
                    V.tensor_tensor(v4(eb), v4(eb), q, ALU.mult).then_inc(lmul, 1)
                e0 = le + 5 + (1 if nl else 0)
                dve.wait_ge(lexp, e0)
                V.tensor_tensor(v4(ek), v4(ek), k_, ALU.mult).then_inc(lmul, 1)
                for l in range(nl):
                    f, lv, _ = halves(l)
                    dve.wait_ge(lexp, e0 + l + 1)
                    V.tensor_tensor(lv[:, :, :, 1, :], lv[:, :, :, 1, :], f(q)[:, :, :, 1, :], ALU.mult).then_inc(lmul, 1)
                    V.tensor_tensor(lv[:, :, :, 0, :], lv[:, :, :, 0, :], f(k_)[:, :, :, 0, :], ALU.mult).then_inc(lmul, 1)
                if nl:
                    for h in range(4):
                        ps = (P23 if h % 2 == 0 else P01)
                        m = msk[h % 2].rearrange("p (l t) -> p l t", l=8)[0:T, 0:nl + 1, 0:T]
                        dve.wait_ge(lmm, count_before(n_lmm, ci) + h + 1)
                        V.tensor_tensor(m, ps[0:T, :].rearrange("p (l t) -> p l t", l=8)[:, 0:nl + 1, 0:T],
                                        mask[0:T, 0:nl + 1, 0:T], ALU.mult).then_inc(at_done, 1)
                        dve.wait_ge(at_done, at + 2 * h + 1)
                        if h >= 2:
                            dve.wait_ge(o_mm, count_before(n_lmm, ci) + h - 1)
                        V.tensor_reduce(AT[h % 2][0:T, 0:T], m.rearrange("p l t -> p t l"), AX_X,
                                        ALU.add).then_inc(at_done, 1)
                dve.wait_ge(s_mm, count_before(n_smm, ci) + 1)
                if ci == 0:
                    V.tensor_copy(S[:].rearrange("p h v -> p (h v)"), b5[:]).then_inc(s_done, 1)
                else:
                    for h in range(4):
                        V.scalar_tensor_tensor(out=S[:, h, :], in0=S[:, h, :], scalar=dec[:, h:h + 1],
                                               in1=b5[:, h * P:(h + 1) * P], op0=ALU.mult, op1=ALU.add).then_inc(s_done, 1)
                if nl:
                    dve.wait_ge(on_done, count_before(n_on, ci) + 3)
                    V.tensor_tensor(ors[:, 0:4 * T], ors[:, 0:4 * T], b4[:, 0:4 * T], ALU.mult).then_inc(mo_done, 1)
                    dve.wait_ge(mo_done, count_before(n_mo, ci) + 1)
                    V.tensor_tensor(mix[:, 0:4, c0:c0 + T], v4(ors), G, ALU.mult).then_inc(mo_done, 1)

            def w_out(g):
                n = N[g]
                dve.sem_inc(h_free[g], 2)
                with dve.Fori(0, B_OUT // WSLOTS) as k:
                    for r in range(WSLOTS):
                        dve.wait_ge(blocks_done, k * WSLOTS + (g * B_ALL + B_IN + r + 1))
                        h = hTf[:, bass.ds(k * (WSLOTS * NMAX) + r * NMAX, n)]
                        V.tensor_tensor(h, h, P01[:, r % 2 * 512:r % 2 * 512 + n], ALU.add).then_inc(h_free[g], 1)

            def choose(s, s0):
                par = s0 % 2
                base = s * TK
                n = [0]

                def did(ins):
                    ins.then_inc(topk, 1)
                    n[0] += 1
                    return n[0]

                def need(v):
                    dve.wait_ge(topk, base + v)
                    own(dve)

                dve.wait_ge(staged, s + 1)
                st = stg[:, par]
                if s0 >= 1:
                    dve.wait_ge(topk, base)
                own(dve)
                for a in range(2):
                    did(V.max(sv[:, a, 0:8], st[:, a, :]))
                for a in range(2):
                    need(1 + a)
                    did(V.max_index(si[:, a, 0:8], sv[:, a, 0:8], st[:, a, :]))
                for a in range(2):
                    did(V.match_replace(rest[:, a, :], sv[:, a, 0:8], st[:, a, :], NEG))
                for a in range(2):
                    need(5 + a)
                    did(V.max(sv[:, a, 8:16], rest[:, a, :]))
                for a in range(2):
                    need(7 + a)
                    did(V.max_index(si[:, a, 8:16], sv[:, a, 8:16], rest[:, a, :]))
                c3 = cand[:].rearrange("p (i j) -> p i j", i=TOPK)
                did(V.tensor_tensor(c3, sv[:, 0, :].unsqueeze(2).broadcast_to([P, TOPK, TOPK]),
                                    sv[:, 1, :].unsqueeze(1).broadcast_to([P, TOPK, TOPK]), ALU.add))
                if s0 >= 2:
                    dve.wait_ge(exp_done, (s - 1) * 2)
                need(11)
                did(V.max(top[:, par, 0:8], cand[:]))
                need(12)
                did(V.match_replace(rest[:].rearrange("p a n -> p (a n)"), top[:, par, 0:8], cand[:], NEG))
                did(V.max_index(pos[:, 0:8], top[:, par, 0:8], cand[:]))
                need(13)
                did(V.max(top[:, par, 8:16], rest[:].rearrange("p a n -> p (a n)")))
                need(15)
                did(V.max_index(pos[:, 8:16], top[:, par, 8:16], rest[:].rearrange("p a n -> p (a n)")))
                need(16)
                did(V.tensor_scalar(hilo[:, 0, :], pos[:], 4, None, ALU.logical_shift_right))
                did(V.tensor_scalar(hilo[:, 1, :], pos[:], 15, None, ALU.bitwise_and))
                need(18)
                did(V.tensor_tensor(onehot[:], hilo[:].unsqueeze(3).broadcast_to([P, 2, TOPK, TOPK]),
                                    iota16.unsqueeze(1).unsqueeze(1).broadcast_to([P, 2, TOPK, TOPK]),
                                    ALU.is_equal))
                need(19)
                did(V.tensor_tensor(onehot[:], onehot[:], si[:].unsqueeze(2).broadcast_to([P, 2, TOPK, TOPK]),
                                    ALU.mult))
                need(20)
                did(V.tensor_reduce(ab[:], onehot[:], AX_X, ALU.add))
                need(21)
                if s0 >= 2:
                    dve.wait_ge(idx_copied, s - 1)
                did(V.scalar_tensor_tensor(out=idxU[:, par, :], in0=ab[:, 0, :], scalar=float(NKEYS), in1=ab[:, 1, :],
                                           op0=ALU.mult, op1=ALU.add))
                assert n[0] == TK

            def first(s):
                choose(s, s)

            def step(s, s0, do_u, do_v, nxt):
                if do_v:
                    par = 1 - s0 % 2
                    dve.wait_ge(exp_done, s * 2)
                    V.reciprocal(exs[:, par, 2:3], exs[:, par, 1:2]).then_inc(w_done, 1)
                    dve.wait_ge(w_done, s * 2 - 1)
                    dve.wait_ge(gelu_done, s)
                    V.scalar_tensor_tensor(out=wgt[:, par, :], in0=ge[:, par, :], scalar=exs[:, par, 2:3],
                                           in1=ex[:, par, :], op0=ALU.mult, op1=ALU.mult).then_inc(w_done, 1)
                if nxt:
                    choose(s + 1, s0 + 1)
                if do_u:
                    x = xtok[TILES[tile_of(s0)][0]]
                    for j in range(TOPK):
                        dve.wait_ge(u_in[j % RU], s * 32 + 16 * (j // RU + 1))
                        V.tensor_tensor_reduce(out=Ur[:, j % RU, :], in0=Ur[:, j % RU, :], in1=x, scale=1.0, scalar=0.0,
                                               op0=ALU.mult, op1=ALU.add,
                                               accum_out=adot[:, s0 % 2, j:j + 1]).then_inc(u_free, 1)

            def y_sum_(i):
                name = TILES[i][0]
                rows = SAMP if name == "pk" else P
                dve.wait_ge(acc_close, i + 1)
                for k, acc in enumerate((b6, b7)):
                    h = htok[name][0:rows, k * 512:(k + 1) * 512]
                    V.tensor_tensor(h, h, acc[0:rows, :], ALU.add).then_inc(y_sum, 1)

            def y_out(i):
                name = TILES[i][0]
                rows = SAMP if name == "pk" else P
                dve.wait_ge(y_rstd, 3 * i + 3)
                h = htok[name][0:rows, :]
                V.scalar_tensor_tensor(out=h, in0=h, scalar=yst[0:rows, 2:3], in1=nf[0:rows, :],
                                       op0=ALU.mult, op1=ALU.mult).then_inc(y_done, 1)

            dve.wait_ge(const_in, 16 * 9)
            dve.wait_ge(const_set, 3)
            dve.sem_inc(u_free, RU)
            run(dve, {"norm": norm, "prep": prep, "chunk": chunk, "w_out": w_out, "first": first, "step": step,
                      "y_sum": y_sum_, "y_out": y_out})

        @block.tensor
        def _(pe):
            M = nc.tensor.matmul

            def norm(g, k):
                n = N[g]
                for c in range(DC):
                    pe.wait_ge(sq_done[g][k], c + 1)
                    M(P23[:, 512:512 + n], ones[:], sqb[c % 2][:, 0:n], start=(c == 0),
                      stop=(c == DC - 1)).then_inc(ss_done[g][k], 1)

            def block_of(g, k, B0, r, src, free):
                n = N[g]
                pe.wait_ge(w_in[r], k * 16 + 16 * ((g * B_ALL + B0) // WSLOTS + 1))
                pe.wait_ge(free, k * WSLOTS + (r + 1))
                for c in range(DC):
                    last = M(P01[:, r % 2 * 512:r % 2 * 512 + n], wring[:, r, c * P:(c + 1) * P], src[:, c, 0:n],
                             start=(c == 0), stop=(c == DC - 1))
                last.then_inc(blocks_done, 1)

            def proj(g):
                pe.wait_ge(xn_done[g][0], DC)
                with pe.Fori(0, B_IN // WSLOTS) as k:
                    for r in range(WSLOTS):
                        block_of(g, k, 0, r, mix, z_free[g])

            def prep(g):
                n, w = N[g], slice(PAD, PAD + N[g])
                pe.wait_ge(pool_step[g], PL[g])
                for i in range(4):
                    if i >= 2:
                        pe.wait_ge(pool_out[g], i - 1)
                    M(P23[:, i % 2 * 512:i % 2 * 512 + n], pw[:, i, :], bufs[i % 2][:, i, w], start=True,
                      stop=True).then_inc(pool_mm[g], 1)

            def chunk(ci):
                g, c0, T, nl, stream = CHUNKS[ci]
                cs = slice(PAD + c0, PAD + c0 + T)
                S = Sp if stream == "p" else Ss
                if ci:
                    pe.wait_ge(mo_done, count_before(n_mo, ci))
                    pe.wait_ge(s_done, count_before(n_sd, ci))
                for h in range(4):
                    last = nc.tensor.transpose(b4[0:T, h * P:(h + 1) * P], z[:, SI, h, cs], ident[:])
                last.then_inc(ctr, 1)
                pe.wait_ge(lmul, count_before(n_lmul, ci) + 1 + (1 if nl else 0))
                for h in range(4):
                    last = nc.tensor.transpose(b5[0:T, h * P:(h + 1) * P], ek[:, h * T:(h + 1) * T], ident[:])
                last.then_inc(ctr, 1)

                def levels(h):
                    ps = (P23 if h % 2 == 0 else P01)
                    if h == 0:
                        pe.wait_ge(lmul, count_before(n_lmul, ci + 1))
                    if h >= 2:
                        pe.wait_ge(at_done, count_before(n_at, ci) + 2 * (h - 2) + 1)
                    M(ps[0:T, 0:T], z[:, SP_, h, cs], z[:, SQ, h, cs], start=True, stop=True)
                    for l in range(nl):
                        m = lev[:, (l * 4 + h) * T:(l * 4 + h + 1) * T]
                        last = M(ps[0:T, (l + 1) * P:(l + 1) * P + T], m, m, start=True, stop=True)
                    last.then_inc(lmm, 1)

                def outputs(h):
                    pe.wait_ge(at_done, count_before(n_at, ci) + 2 * h + 2)
                    o = b4[:, h * T:(h + 1) * T]
                    M(o, vtok[0:T, h * P:(h + 1) * P], AT[h % 2][0:T, 0:T], start=True, stop=False)
                    M(o, S[:, h, :], eb[:, h * T:(h + 1) * T], start=False, stop=True).then_inc(o_mm, 1)

                if nl:
                    levels(0)
                    levels(1)
                    pe.wait_ge(ctr_out, count_before(n_ctr, ci) + 1)
                    outputs(0)
                    levels(2)
                    outputs(1)
                    levels(3)
                    outputs(2)
                    outputs(3)
                pe.wait_ge(ctr_out, count_before(n_ctr, ci) + 2)
                for h in range(4):
                    last = M(b5[:, h * P:(h + 1) * P], ktok[0:T, h * P:(h + 1) * P], vtok[0:T, h * P:(h + 1) * P],
                             start=True, stop=True)
                last.then_inc(s_mm, 1)
                if nl:
                    pe.wait_ge(on_done, count_before(n_on, ci) + 1)
                    M(P23[:, 0:4 * T], ones[:], osq[:, 0:4 * T], start=True, stop=True).then_inc(osum_done, 1)

            def w_out(g):
                pe.wait_ge(mo_done, count_before(n_mo, 3 if g == 0 else 6))
                pe.wait_ge(pool_out[g], 4)
                with pe.Fori(0, B_OUT // WSLOTS) as k:
                    for r in range(WSLOTS):
                        block_of(g, k, B_IN, r, mix, h_free[g])

            def tok(g):
                u = 0
                for src, name_ in ((hT, "h"), (xn2, "x")):
                    if name_ == "x":
                        pe.wait_ge(xn_done[g][1], DC)
                    for name, c0 in group_tiles[g]:
                        for half in range(2):
                            if u >= 2:
                                pe.wait_ge(tr_out[g], u - 1)
                            for c in range(4):
                                dst = TB[u % 2][:, c * P:(c + 1) * P]
                                blk = src[:, half * 4 + c, c0:c0 + (SAMP if name == "pk" else P)]
                                if name != "pk":
                                    last = nc.tensor.transpose(dst, blk, ident[:])
                                elif name_ == "h":
                                    last = nc.tensor.transpose(dst[0:SAMP, :], blk, ident[:])
                                else:
                                    for q in range(4):
                                        last = M(dst[SAMP * q:SAMP * (q + 1), :], blk, ident[:], start=True, stop=True)
                            last.then_inc(tr_mm[g], 1)
                            u += 1

            def query(g):
                with pe.Fori(0, B_Q // WSLOTS) as k:
                    def project(r):
                        block_of(g, k, B_IN + B_OUT, r, xn2, q_free[g])

                    def scores(r):
                        pe.wait_ge(q_free[g], k * WSLOTS + (2 + r + 1))
                        pe.wait_ge(sc_free[g], k * WSLOTS + (r + 1))
                        o = r % 2 * 512
                        for i, (name, c0) in enumerate(group_tiles[g]):
                            if name == "pk":
                                last = M(P23[SAMP * r:SAMP * (r + 1), o + i * P:o + (i + 1) * P], qT[r % 2][:, c0:c0 + SAMP],
                                         wring[:, r, D:WQ], start=True, stop=True)
                            else:
                                last = M(P23[:, o + i * P:o + (i + 1) * P], qT[r % 2][:, c0:c0 + P], wring[:, r, D:WQ],
                                         start=True, stop=True)
                        last.then_inc(sc_mm[g], 1)

                    project(0)
                    project(1)
                    scores(0)
                    project(2)
                    scores(1)
                    project(3)
                    scores(2)
                    scores(3)

            def step(s, s0, do_u, do_v, nxt):
                if not do_v:
                    return
                i = tile_of(s0 - 1)
                name, t0, tn = TILES[i]
                m = SAMP if name == "pk" else P
                if s0 - 1 == t0:
                    if i:
                        pe.wait_ge(y_sum, 2 * i)
                    for acc in (b6, b7):
                        M(acc[0:m, :], zb[0:1, 0:m], zb[0:1, :], start=True, stop=False)
                for j in range(TOPK):
                    pe.wait_ge(v_in[j % RV], (s - 1) * 64 + 16 * (j // RV + 1))
                    pe.wait_ge(diag_done, (s - 1) * TOPK + j + 1)
                    for k, acc in enumerate((b6, b7)):
                        last = M(acc[0:m, :], diag[:, j % RD, 0:m], Vr[:, j % RV, k * 512:(k + 1) * 512], start=False,
                                 stop=False)
                    last.then_inc(v_free, 1)
                if s0 == t0 + tn:
                    for acc in (b6, b7):
                        last = M(acc[0:m, :], zb[0:1, 0:m], zb[0:1, :], start=False, stop=True)
                    last.then_inc(acc_close, 1)

            pe.wait_ge(const_in, 16 * 9)
            pe.wait_ge(const_set, 3)
            pe.sem_inc(v_free, RV)
            run(pe, {"norm": norm, "proj": proj, "prep": prep, "chunk": chunk, "w_out": w_out, "tok": tok,
                     "query": query, "step": step})


def kernel(**inputs):
    import numpy as np
    import concourse.bacc as bacc
    from concourse.bass_utils import run_bass_kernel_spmd

    a = {k: np.asarray(v) for k, v in inputs.items()}
    f32 = np.float32
    blocks = lambda w: w.reshape(DC, P, -1)
    x = a["x_prompt"][0]
    xcols = np.concatenate([a["meta_tokens"], x[:P], np.zeros((GAP, D), f32), a["x_sample"][0], x[P:]], axis=0)
    xT = xcols.T.reshape(DC, P, COLS).transpose(1, 0, 2)

    def weight_blocks(w):
        return w.reshape(DC, P, -1, P).transpose(2, 1, 0, 3).reshape(-1, P, DC * P)

    w_io = np.concatenate([weight_blocks(a["w_in"][0]), weight_blocks(a["w_out"][0])], axis=0)
    order = [(2 * r + (k >> 1)) * 2 + (k & 1) for k in range(4) for r in range(4)]
    subk = a["peer_subkeys"][0].reshape(B_Q, NKEYS, P).transpose(0, 2, 1)
    w_q = np.concatenate([weight_blocks(a["peer_w_query"][0])[order], subk[order]], axis=2)
    fm = lambda v: v.reshape(-1, P).T
    lg = a["hgrn_lb_logits"]
    vecs = np.concatenate([fm(a["norm_mix"][0]), fm(a["norm_ffn"][0]), fm(a["hgrn_out_norm"][0]),
                           fm(a["pool_scale"][0]), fm(lg[0]), fm(lg[1])], axis=1)
    t = np.arange(P)
    masks = np.zeros((P, 8, P), f32)
    masks[:, 0, :] = t[:, None] == t[None, :]
    for l in range(7):
        same = (t[:, None] >> (l + 1)) == (t[None, :] >> (l + 1))
        masks[:, l + 1, :] = same & ((t[:, None] >> l) % 2 == 0) & ((t[None, :] >> l) % 2 == 1)
    small = np.zeros((P, 80), f32)
    small[:, 0:16] = np.arange(16)
    for i, w in enumerate(WINDOWS):
        small[:, 16 + 16 * i:32 + 16 * i] = w / np.minimum(w, np.arange(META) + 1.0)
    arrays = {
        "xT": xT, "w_io": w_io, "w_q": w_q, "pool_w": a["pool_w"][0].transpose(1, 0, 2), "vecs": vecs, "masks": masks,
        "ident": np.eye(P, dtype=f32), "sel": np.tile(np.eye(SAMP, dtype=f32), (4, 1)), "small": small,
        "cacheT": a["cache_pool"][0, 0].T.reshape(4, P, HIST).transpose(1, 0, 2),
        "state": a["state_hgrn"][0, 0].transpose(1, 0, 2), "nf": a["norm_final"],
        "peer_u": a["peer_u"][0], "peer_v": a["peer_v"][0],
    }
    arrays = {k: np.ascontiguousarray(v) for k, v in arrays.items()}
    outs = {"y_prompt": (SEQ, D), "y_sample": (SAMP, D), "sp": (P, 4, P), "ss": (P, 4, P), "cp": (P, 4, HIST),
            "cs": (P, 4, HIST)}
    nc = bacc.Bacc("TRN2", target_bir_lowering=False, num_devices=1)
    args = [nc.dram_tensor("in_" + k, v.shape, FP32, kind="ExternalInput").ap() for k, v in arrays.items()]
    args += [nc.dram_tensor("out_" + k, s, FP32, kind="ExternalOutput").ap() for k, s in outs.items()]
    build(nc, *args)
    r = run_bass_kernel_spmd(nc, [{"in_" + k: v for k, v in arrays.items()}], core_ids=[0]).results[0]
    o = {k: r["out_" + k] for k in outs}
    st = lambda s: s.transpose(1, 0, 2)[None, None]
    hist = lambda c: c.transpose(2, 1, 0).reshape(HIST, 4 * P)[None, None]
    return (o["y_prompt"][None], o["y_sample"][None], st(o["sp"]), hist(o["cp"]), st(o["ss"]), hist(o["cs"]))
```

```python
import concourse.bass as bass
from concourse import mybir
from contextlib import ExitStack

FP32 = mybir.dt.float32
BF16 = mybir.dt.bfloat16
U32 = mybir.dt.uint32
ALU = mybir.AluOpType
ACT = mybir.ActivationFunctionType
AX_X = mybir.AxisListType.X

P = 128
D = 1024
DC = D // P
SEQ, META, SAMP = 512, 16, 32
H_A = 4
HIST = 15
WINDOWS = (2, 4, 8, 16)
PEER_H, TOPK, NKEYS = 8, 16, 128
EPS = 1e-6
NEG = -3.0e38

GAP = 16
N = (META + P + GAP + SAMP, SEQ - P)
COLS = sum(N)
SAMP0 = META + P + GAP
NMAX = max(N)
PAD = 16
ZW = NMAX + PAD
CHUNKS = [(0, 0, META, 0, "p"), (0, META, P, 7, "p"), (0, SAMP0, SAMP, 5, "s"),
          (1, 0, P, 7, "p"), (1, P, P, 7, "p"), (1, 2 * P, P, 7, "p")]

B_IN, B_OUT, B_Q = 20, 8, 16
B_ALL = B_IN + B_OUT + B_Q
WSLOTS = 4
WQ = D + NKEYS

TILES = [("t0", 0, 8), ("pk", 8, 2), ("t1", 10, 8), ("t2", 18, 8), ("t3", 26, 8)]
STEPS = 34
G0_STEPS = 10
RU, RV = 8, 4
QUARTER_IDLE, QUARTER_EMPTY = 7.5, 12.0


def count_before(per_chunk, chunk):
    return sum(per_chunk(c) for c in CHUNKS[:chunk])


def build(nc, xT, w_io, w_q, pool_w, vecs, masks, ident_d, sel_d, small_d, cacheT, state_d, nf_d, peer_u, peer_v,
          y_prompt, y_sample, sp_out, ss_out, cp_out, cs_out):
    ctx = ExitStack()
    with ctx:
        def sb(name, shape, dt=FP32):
            return ctx.enter_context(nc.sbuf_tensor(name, shape, dt))

        def sem(name):
            return ctx.enter_context(nc.semaphore(name))

        hT = sb("hT", [P, DC, NMAX])
        mix = sb("mix", [P, DC, NMAX])
        S_FLOATS = G0_STEPS * 2 * NKEYS
        arena = sb("arena", [P, S_FLOATS + 20 * ZW])
        lev = sb("lev", [P, 7 * 4 * P])
        wring = sb("wring", [P, WSLOTS, WQ])
        mask = sb("mask", [P, 8, P])
        nf = sb("nf", [P, D])
        ident = sb("ident", [P, P])
        sel = sb("sel", [P, SAMP])
        ones = sb("ones", [P, P])
        small = sb("small", [P, 16 + 4 * 16])
        pw = sb("pw", [P, 4, P])
        vec = sb("vec", [P, 40])
        lbt = sb("lbt", [P, 12])
        epst = sb("epst", [P, 1])
        cache = sb("cache", [P, 4, HIST])
        carry = sb("carry", [P, 4, HIST])
        cs_buf = sb("cs_buf", [P, 4, HIST])
        cp_buf = sb("cp_buf", [P, 4, HIST])
        Sp = sb("Sp", [P, 4, P])
        Ss = sb("Ss", [P, 4, P])
        htok0 = sb("htok0", [P, D])
        htoks = sb("htoks", [SAMP, D])
        xtok0 = sb("xtok0", [P, D])
        xtokp = sb("xtokp", [P, D])
        Ur = sb("Ur", [P, RU, D])
        Vr = sb("Vr", [P, RV, D])
        ctmp = sb("ctmp", [P, 2 * 8 * P + 2 * P + 4 * 4 * P])
        dec = sb("dec", [P, 4])
        stg = sb("stg", [P, 2, 2, NKEYS])
        rest = sb("rest", [P, 2, NKEYS])
        cand = sb("cand", [P, TOPK * TOPK])
        onehot = sb("onehot", [P, 2, TOPK, TOPK])
        sv = sb("sv", [P, 2, TOPK])
        si = sb("si", [P, 2, TOPK], U32)
        top = sb("top", [P, 2, TOPK])
        pos = sb("pos", [P, TOPK], U32)
        hilo = sb("hilo", [P, 2, TOPK], U32)
        ab = sb("ab", [P, 2, TOPK])
        idxU = sb("idxU", [P, 2, TOPK], U32)
        idxV = sb("idxV", [P, 2, TOPK], U32)
        ex = sb("ex", [P, 2, TOPK])
        exs = sb("exs", [P, 2, 4])
        adot = sb("adot", [P, 2, TOPK])
        ge = sb("ge", [P, 2, TOPK])
        wgt = sb("wgt", [P, 2, TOPK])
        diag = sb("diag", [P, RV, P])
        ydump = sb("ydump", [P, D], BF16)
        yst = sb("yst", [P, 4])
        zb = sb("zb", [1, 512], BF16)

        nw = (vec[:, 0:8], vec[:, 8:16])
        onorm, pscale, lg = vec[:, 16:20], vec[:, 20:24], vec[:, 24:32]
        lb, oml = lbt[:, 0:4], lbt[:, 4:8]
        iota16, rcnt = small[:, 0:16], small[:, 16:80].rearrange("p (g t) -> p g t", g=4)
        zf_ = arena[:, S_FLOATS:S_FLOATS + 20 * ZW]
        z = zf_.rearrange("p (s h c) -> p s h c", s=5, h=4)
        SQ, SF, SI, SG, SP_ = range(5)
        bufs = [lev[:, 0:4 * ZW].rearrange("p (g c) -> p g c", g=4),
                lev[:, 4 * ZW:8 * ZW].rearrange("p (g c) -> p g c", g=4)]
        xn2 = lev[:, 0:DC * NMAX].rearrange("p (c n) -> p c n", c=DC)
        msk = [ctmp[:, i * 1024:(i + 1) * 1024] for i in range(2)]
        AT = [ctmp[:, 2048 + i * P:2048 + (i + 1) * P] for i in range(2)]
        o4 = 2048 + 2 * P
        eb, ek, vtok, ktok = [ctmp[:, o4 + i * 512:o4 + (i + 1) * 512] for i in range(4)]
        osq, ors = [msk[0][:, i * 512:(i + 1) * 512] for i in range(2)]
        sqb = [ctmp[:, i * NMAX:(i + 1) * NMAX] for i in range(2)]
        rst = ctmp[:, 2 * NMAX:3 * NMAX]
        qT = [ctmp[:, (3 + i) * NMAX:(4 + i) * NMAX] for i in range(2)]
        htok = {"t0": htok0[:], "pk": htoks[:]}
        xtok = {"t0": xtok0[:], "pk": xtokp[:]}
        mixf, hTf = mix[:].rearrange("p c n -> p (c n)"), hT[:].rearrange("p c n -> p (c n)")
        for i in range(3):
            htok[f"t{i + 1}"] = mixf[:, i * D:(i + 1) * D]
            xtok[f"t{i + 1}"] = hTf[:, i * D:(i + 1) * D]

        P01 = ctx.enter_context(nc.psum_tensor("P01", [P, 1024], FP32))
        P23 = ctx.enter_context(nc.psum_tensor("P23", [P, 1024], FP32))
        b4, b5, b6, b7 = [ctx.enter_context(nc.psum_tensor(f"b{i}", [P, 512], FP32)) for i in (4, 5, 6, 7)]
        TB = (b4, b5)

        x_in = [sem(f"x_in{g}") for g in range(2)]
        const_in, const_set = sem("const_in"), sem("const_set")
        w_in = [sem(f"w_in{r}") for r in range(WSLOTS)]
        blocks_done = sem("blocks_done")
        lb_diff, lb_set = sem("lb_diff"), sem("lb_set")
        sq_done = [[sem(f"sq_done{g}{k}") for k in range(2)] for g in range(2)]
        ss_done = [[sem(f"ss_done{g}{k}") for k in range(2)] for g in range(2)]
        xn_done = [[sem(f"xn_done{g}{k}") for k in range(2)] for g in range(2)]
        z_free = [sem(f"z_free{g}") for g in range(2)]
        h_free = [sem(f"h_free{g}") for g in range(2)]
        q_free = [sem(f"q_free{g}") for g in range(2)]
        pool_step = [sem(f"pool_step{g}") for g in range(2)]
        pool_mm = [sem(f"pool_mm{g}") for g in range(2)]
        pool_out = [sem(f"pool_out{g}") for g in range(2)]
        act_prep = [sem(f"act_prep{g}") for g in range(2)]
        dve_prep = [sem(f"dve_prep{g}") for g in range(2)]
        lsub, lexp, lmul, ctr, ctr_out, lmm, at_done, o_mm, s_mm, s_done, on_done, osum_done, mo_done = [
            sem(n) for n in ("lsub", "lexp", "lmul", "ctr", "ctr_out", "lmm", "at_done", "o_mm", "s_mm", "s_done",
                             "on_done", "osum_done", "mo_done")]
        tr_mm = [sem(f"tr_mm{g}") for g in range(2)]
        tr_out = [sem(f"tr_out{g}") for g in range(2)]
        sc_mm = [sem(f"sc_mm{g}") for g in range(2)]
        sc_free = [sem(f"sc_free{g}") for g in range(2)]
        staged, topk, exp_done, gelu_done, w_done, diag_done = [sem(n) for n in (
            "staged", "topk", "exp_done", "gelu_done", "w_done", "diag_done")]
        diag3_done = sem("diag3_done")
        idx_copied = sem("idx_copied")
        u_free, v_free, v3_free = sem("u_free"), sem("v_free"), sem("v3_free")
        u_in = [sem(f"u_in{r}") for r in range(RU)]
        v_in = [sem(f"v_in{r}") for r in range(RV)]
        acc_open, acc_close, y_sum, y_rstd, y_done, stored = [sem(n) for n in (
            "acc_open", "acc_close", "y_sum", "y_rstd", "y_done", "stored")]

        full = lambda c: 1 if c[3] else 0
        n_lsub = lambda c: 2 * c[3]
        n_lexp = lambda c: 5 + full(c) + c[3]
        n_lmul = lambda c: 1 + full(c) + 2 * c[3]
        n_ctr = lambda c: 2
        n_lmm = lambda c: 4 * full(c)
        n_at = lambda c: 8 * full(c)
        n_smm = lambda c: 1
        n_sd = lambda c: 1 if not full(c) else 4
        n_on = lambda c: 3 * full(c)
        n_os = lambda c: full(c)
        n_mo = lambda c: 2 * full(c)
        PL = ((16, 10))
        DP_K, DP_G = 5, 9
        n_scans = lambda g: 4 * sum(1 for c in CHUNKS if c[0] == g)
        group_tiles = ((("t0", META), ("pk", SAMP0)), (("t1", 0), ("t2", P), ("t3", 2 * P)))
        n_tr = (8, 12)
        TK = 22

        waited = {n: sem(f"waited_{n}") for n in ("vector", "gpsimd")}

        def tok_unit(g, u):
            per = 2 * len(group_tiles[g])
            return u >= per, group_tiles[g][u % per // 2], u % 2

        def own(eng):
            eng.sem_inc(waited["gpsimd" if eng is nc.gpsimd else "vector"], 1)

        def trunk(g):
            parts = [(8, ("norm", g, 0))] + [(5.2, ("proj", g, j)) for j in range(B_IN)] + [(10, ("prep", g))]
            for c in range(len(CHUNKS)):
                if CHUNKS[c][0] == g:
                    parts += [(t, (n, c)) for t, n in ((8, "decay"), (6, "heads01"), (6, "heads23"), (4, "state"))]
            parts += [(5.2, ("w_out", g, j)) for j in range(B_OUT)] + [(8, ("norm", g, 1))]
            parts += [(1, ("tok", g, u)) for u in range(n_tr[g])] + [(6, ("query", g, j)) for j in range(B_Q + 1)]
            return parts

        def steps(first, last, between=()):
            between, out = list(between), [("first", first)]
            room = 0.0
            ends = {t[1] + t[2]: i for i, t in enumerate(TILES)}
            s = first
            while s <= last:
                go, nxt = s < last, s + 1 < last
                for quarter in range(4):
                    out.append(("step", s, s, quarter, go, s > first, nxt))
                    room += QUARTER_IDLE if s > first else QUARTER_EMPTY
                    while between and room >= between[0][0]:
                        room -= between[0][0]
                        out.append(between.pop(0)[1])
                if s in ends and s > first:
                    out.append(("y_sum", ends[s]))
                if s - 1 in ends and s - 1 > first:
                    out.append(("y_out", ends[s - 1]))
                s += 1
                in_tile = [t for t in TILES if t[1] < s < t[1] + t[2]]
                if not between and in_tile and s == in_tile[0][1] + 2 and in_tile[0][2] == 8:
                    pairs = 2 if in_tile[0][1] + 8 == last else 3
                    out.append(("loop", s, pairs))
                    s += 2 * pairs
            return out + [("y_out", ends[last])] + [x for _, x in between]

        plan = [x for _, x in trunk(0)] + steps(0, G0_STEPS, trunk(1)) + steps(G0_STEPS, STEPS)

        def tile_of(s):
            return [i for i, t in enumerate(TILES) if t[1] <= s < t[1] + t[2]][0]

        def run(eng, parts):
            i = 0
            while i < len(plan):
                kind, *a = plan[i]
                i += 1
                if kind == "loop":
                    s0, pairs = a
                    with eng.Fori(0, pairs) as k:
                        for par in range(2):
                            for quarter in range(4):
                                if "step" in parts:
                                    parts["step"](k * 2 + (s0 + par), s0 + par, quarter, True, True, True)
                elif kind in ("proj", "w_out", "query"):
                    if kind not in parts:
                        continue
                    g, j = a
                    n = 0
                    while j % 4 == 0 and i + n < len(plan) and plan[i + n][0] == kind:
                        n += 1
                    turns = (n + 1) // 4
                    if j == 0:
                        parts[kind](g, None, 0)
                    if turns >= 2 and kind != "query":
                        with eng.Fori(j // 4, j // 4 + turns) as k:
                            for r in range(4):
                                parts[kind](g, k, r)
                        i += 4 * turns - 1
                    else:
                        parts[kind](g, j // 4, j % 4)
                elif kind in parts:
                    parts[kind](*a)

        block = ctx.enter_context(nc.Block())

        def ysteps(sp, a, b):
            for i in range(a, b):
                name = TILES[i][0]
                sp.wait_ge(y_done, i + 1)
                if name == "pk":
                    sp.dma_start(y_sample, htok[name]).then_inc(stored, 16)
                else:
                    n = int(name[1])
                    sp.dma_start(y_prompt[n * P:(n + 1) * P, :], htok[name]).then_inc(stored, 16)

        @block.sync
        def _(sp):
            sp.dma_start(hT[:, :, 0:N[0]], xT[:, :, 0:N[0]]).then_inc(x_in[0], 16)
            for dst, src in ((vec[:, 0:32], vecs), (small[:], small_d), (ident[:], ident_d), (pw[:], pool_w),
                             (mask[:], masks), (cache[:], cacheT), (Ss[:], state_d), (sel[:], sel_d),
                             (nf[:], nf_d.partition_broadcast(P))):
                sp.dma_start(dst, src).then_inc(const_in, 16)

            def load(B, r, query):
                if query:
                    sp.dma_start(wring[:, r, :], w_q[bass.ds(B, 1), :, :].rearrange("b p m -> p (b m)")
                                 ).then_inc(w_in[r], 16)
                else:
                    sp.dma_start(wring[:, r, 0:D], w_io[bass.ds(B, 1), :, :].rearrange("b p m -> p (b m)")
                                 ).then_inc(w_in[r], 16)

            for g in range(2):
                base = g * B_ALL
                if g:
                    sp.wait_ge(tr_out[0], n_tr[0])
                    sp.wait_ge(xn_done[0][1], DC)
                    sp.dma_start(hT[:, :, 0:N[1]], xT[:, :, N[0]:COLS]).then_inc(x_in[1], 16)
                for r in range(WSLOTS):
                    if g:
                        sp.wait_ge(blocks_done, base + r - 1)
                    load(r, r, False)
                with sp.Fori(1, (B_IN + B_OUT) // WSLOTS) as k:
                    for r in range(WSLOTS):
                        sp.wait_ge(blocks_done, k * WSLOTS + (base + r + 1 - WSLOTS))
                        load(k * WSLOTS + r, r, False)
                for r in range(WSLOTS):
                    sp.wait_ge(blocks_done, base + B_IN + B_OUT + r + 1 - WSLOTS)
                    load(r, r, True)
                with sp.Fori(1, B_Q // WSLOTS) as k:
                    for r in range(WSLOTS):
                        sp.wait_ge(blocks_done, k * WSLOTS + (base + B_IN + B_OUT + r - 1))
                        load(k * WSLOTS + r, r, True)
            sp.wait_ge(pool_step[1], 2)
            sp.dma_start(cs_out, cs_buf[:]).then_inc(stored, 16)
            sp.dma_start(cp_out, cp_buf[:]).then_inc(stored, 16)
            sp.wait_ge(s_done, count_before(n_sd, 6))
            sp.dma_start(ss_out, Ss[:]).then_inc(stored, 16)
            sp.dma_start(sp_out, Sp[:]).then_inc(stored, 16)
            ysteps(sp, 0, 5)
            sp.wait_ge(stored, 16 * 9)

        @block.gpsimd
        def _(pool):
            nc.gpsimd.memset(ones[:], 1.0).then_inc(const_set, 1)
            nc.gpsimd.memset(epst[:], EPS).then_inc(const_set, 1)
            nc.gpsimd.memset(zb[:], 0.0).then_inc(const_set, 1)

            def step(s, s0, quarter, do_u, do_v, _next):
                par = s0 % 2
                if do_u and quarter == 0:
                    pool.wait_ge(topk, s * TK + TK)
                    own(pool)
                for r in range(4):
                    j = 4 * quarter + r
                    if do_u:
                        pool.wait_ge(u_free, s * TOPK + j + 1)
                        own(pool)
                        pool.indirect_dma_start(Ur[:, j % RU, :], None, peer_u, bass.IndirectOffsetOnAxis(
                            ap=idxU[:, par, j:j + 1], axis=0)).then_inc(u_in[j % RU], 16)
                    if do_v:
                        if j == 0:
                            pool.wait_ge(idx_copied, s)
                        if r < 3:
                            pool.wait_ge(v_free, (s - 1) * 12 + 3 * quarter + r + 1)
                        else:
                            pool.wait_ge(v3_free, (s - 1) * 4 + quarter + 1)
                        own(pool)
                        pool.indirect_dma_start(Vr[:, r, :], None, peer_v, bass.IndirectOffsetOnAxis(
                            ap=idxV[:, 1 - par, j:j + 1], axis=0)).then_inc(v_in[r], 16)
                if do_u and quarter == 3:
                    nc.gpsimd.tensor_copy(idxV[:, par, :], idxU[:, par, :]).then_inc(idx_copied, 1)

            run(pool, {"step": step})

        @block.scalar
        def _(act):
            A = nc.scalar.activation

            def norm(g, k):
                n = N[g]
                if k == 0:
                    act.wait_ge(x_in[g], 16)
                    act.wait_ge(const_set, 2)
                else:
                    act.wait_ge(h_free[g], 2 + DC)
                for c in range(DC):
                    if c >= 2:
                        act.wait_ge(ss_done[g][k], c - 1)
                    A(sqb[c % 2][:, 0:n], hT[:, c, 0:n], ACT.Square).then_inc(sq_done[g][k], 1)
                act.wait_ge(ss_done[g][k], DC)
                A(rst[:, 0:n], P23[:, 512:512 + n], ACT.Ln, scale=1.0 / D, bias=epst[:]).then_inc(sq_done[g][k], 1)
                act.wait_ge(sq_done[g][k], DC + 1)
                A(rst[:, 0:n], rst[:, 0:n], ACT.Exp, scale=-0.5).then_inc(sq_done[g][k], 1)

            def proj(g, k, r):
                if k is None:
                    act.sem_inc(z_free[g], 2)
                    return
                act.wait_ge(blocks_done, k * WSLOTS + (g * B_ALL + r + 1))
                A(zf_[:, bass.ds(k * (WSLOTS * ZW) + (r * ZW + PAD), N[g])], P01[:, r % 2 * 512:r % 2 * 512 + N[g]],
                  ACT.Copy).then_inc(z_free[g], 1)

            def prep(g):
                n, w = N[g], slice(PAD, PAD + N[g])
                tA = lev[:, 0:4 * n].rearrange("p (h c) -> p h c", h=4)
                tB = lev[:, 4 * n:8 * n].rearrange("p (h c) -> p h c", h=4)
                tC = mix[:, 0:4, 0:n]
                if g == 0:
                    act.wait_ge(lb_diff, 1)
                    A(lb, lbt[:, 8:12], ACT.Sigmoid).then_inc(lb_set, 1)
                    A(oml, lbt[:, 8:12], ACT.Sigmoid, scale=-1.0).then_inc(lb_set, 1)
                for i in range(4):
                    act.wait_ge(pool_mm[g], i + 1)
                    A(mix[:, 4 + i, 0:n], P23[:, i % 2 * 512:i % 2 * 512 + n], ACT.Copy,
                      scale=pscale[:, i:i + 1]).then_inc(pool_out[g], 1)
                A(tC, z[:, SQ, :, w], ACT.Sigmoid).then_inc(act_prep[g], 1)
                A(tA, z[:, SF, :, w], ACT.Sigmoid).then_inc(act_prep[g], 1)
                A(tB, z[:, SF, :, w], ACT.Sigmoid, scale=-1.0).then_inc(act_prep[g], 1)
                act.wait_ge(dve_prep[g], DP_K)
                A(tB, z[:, SG, :, w], ACT.Sigmoid).then_inc(act_prep[g], 1)
                act.wait_ge(act_prep[g], 2)
                act.wait_ge(lb_set, 2)
                for h in range(4):
                    A(tA[:, h, :], tA[:, h, :], ACT.Ln, scale=oml[:, h:h + 1], bias=lb[:, h:h + 1]).then_inc(act_prep[g], 1)

            def decay(ci):
                g, c0, T, nl, _ = c = CHUNKS[ci]
                b = z[:, SF, :, PAD + c0:PAD + c0 + T]
                last = b[:, :, T - 1]
                v4 = lambda t: t[:, 0:4 * T].rearrange("p (h t) -> p h t", h=4)
                scans = DP_G + 4 * (1 + sum(1 for x in CHUNKS[:ci] if x[0] == g))
                if ci:
                    act.wait_ge(s_mm, count_before(n_smm, ci))
                act.wait_ge(ctr, count_before(n_ctr, ci) + 1)
                A(vtok[0:T, :], b4[0:T, :], ACT.Copy).then_inc(ctr_out, 1)
                act.wait_ge(dve_prep[g], scans)
                if nl:
                    A(v4(eb), b, ACT.Exp).then_inc(lexp, 1)
                for h in range(4):
                    A(ek[:, h * T:(h + 1) * T], b[:, h, :], ACT.Exp, scale=-1.0, bias=last[:, h:h + 1]).then_inc(lexp, 1)
                A(dec[:], last, ACT.Exp).then_inc(lexp, 1)
                for l in range(nl):
                    act.wait_ge(lsub, count_before(n_lsub, ci) + 2 * l + 2)
                    lv = lev[:, l * 4 * T:(l + 1) * 4 * T]
                    A(lv, lv, ACT.Exp).then_inc(lexp, 1)
                act.wait_ge(ctr, count_before(n_ctr, ci) + 2)
                A(ktok[0:T, :], b5[0:T, :], ACT.Copy).then_inc(ctr_out, 1)

            def state(ci):
                g, c0, T, nl, _ = CHUNKS[ci]
                if nl:
                    act.wait_ge(o_mm, count_before(n_lmm, ci) + 4)
                    A(osq[:, 0:4 * T], b4[:, 0:4 * T], ACT.Square).then_inc(on_done, 1)
                    act.wait_ge(osum_done, count_before(n_os, ci) + 1)
                    A(ors[:, 0:4 * T], P23[:, 0:4 * T], ACT.Ln, scale=1.0 / P, bias=epst[:]).then_inc(on_done, 1)
                    act.wait_ge(on_done, count_before(n_on, ci) + 2)
                    A(ors[:, 0:4 * T], ors[:, 0:4 * T], ACT.Exp, scale=-0.5).then_inc(on_done, 1)

            def tok(g, u):
                is_x, (name, _), half = tok_unit(g, u)
                rows = SAMP if (name == "pk" and not is_x) else P
                act.wait_ge(tr_mm[g], u + 1)
                A((xtok if is_x else htok)[name][0:rows, half * 512:(half + 1) * 512], TB[u % 2][0:rows, :],
                  ACT.Copy).then_inc(tr_out[g], 1)

            def query(g, k, r):
                n = N[g]
                if k is None:
                    act.sem_inc(q_free[g], 2)
                    act.sem_inc(sc_free[g], 2)
                    return
                j = 4 * k + r
                if j < B_Q:
                    act.wait_ge(blocks_done, g * B_ALL + B_IN + B_OUT + j + 1)
                    A(qT[r % 2][:, 0:n], P01[:, r % 2 * 512:r % 2 * 512 + n], ACT.Copy).then_inc(q_free[g], 1)
                if not j:
                    return
                k, r = divmod(j - 1, 4)
                act.wait_ge(sc_mm[g], j)
                o = r % 2 * 512
                at = k * NKEYS + r * 512
                if g:
                    dst = arena[:, S_FLOATS:S_FLOATS + 3 * 2048].rearrange("p (t s) -> p t s", t=3)
                    A(dst[:, :, at:at + NKEYS], P23[:, o:o + 384].rearrange("p (t s) -> p t s", t=3),
                      ACT.Copy).then_inc(sc_free[g], 1)
                else:
                    A(arena[:, at:at + NKEYS], P23[:, o:o + P], ACT.Copy)
                    q, at = slice(SAMP * r, SAMP * (r + 1)), k * NKEYS + 8 * 256
                    A(arena[q, at:at + NKEYS], P23[q, o + P:o + 2 * P], ACT.Copy).then_inc(sc_free[g], 1)

            def stage(s, s0):
                if s0 >= 2:
                    act.wait_ge(topk, (s - 1) * TK)
                A(stg[:, s0 % 2].rearrange("p a n -> p (a n)"), arena[:, bass.ds(s * 256, 256)], ACT.Copy).then_inc(staged, 1)

            def exps(s, s0):
                par = s0 % 2
                act.wait_ge(topk, s * TK + 16)
                if s0 >= 2:
                    act.wait_ge(w_done, (s - 1) * 2)
                A(exs[:, par, 0:1], top[:, par, 0:1], ACT.Copy, scale=-1.0).then_inc(exp_done, 1)
                act.wait_ge(exp_done, s * 2 + 1)
                A(ex[:, par, :], top[:, par, :], ACT.Exp, bias=exs[:, par, 0:1],
                  accum_out=exs[:, par, 1:2]).then_inc(exp_done, 1)

            def first(s):
                if s:
                    act.wait_ge(sc_free[1], 2 + B_Q)
                else:
                    act.wait_ge(sc_free[0], 2 + B_Q)
                stage(s, s)
                exps(s, s)

            def step(s, s0, quarter, do_u, do_v, nxt):
                if nxt and quarter == 0:
                    stage(s + 1, s0 + 1)
                if do_v:
                    par = 1 - s0 % 2
                    if quarter == 0:
                        act.wait_ge(u_free, s * TOPK + RU)
                        A(ge[:, par, :], adot[:, par, :], ACT.Gelu).then_inc(gelu_done, 1)
                        act.wait_ge(w_done, s * 2)
                    packed = TILES[tile_of(s0 - 1)][0] == "pk"
                    for qd in {0: (0, 1), 1: (2,), 2: (3,), 3: ()}[quarter]:
                        for r in range(4 if packed else 3):
                            j = 4 * qd + r
                            if r < 3:
                                act.wait_ge(v_free, (s - 1) * 12 + 3 * qd + r + 1)
                            else:
                                act.wait_ge(v3_free, (s - 1) * 4 + qd + 1)
                            src = sel if packed else ident
                            A(diag[:, r, 0:SAMP if packed else P], src[:], ACT.Copy,
                              scale=wgt[:, par, j:j + 1]).then_inc(diag_done if r < 3 else diag3_done, 1)
                if nxt and quarter == 3:
                    exps(s + 1, s0 + 1)

            def y_sum_(i):
                name = TILES[i][0]
                rows = SAMP if name == "pk" else P
                act.wait_ge(y_sum, 2 * (i + 1))
                A(ydump[0:rows, :], htok[name][0:rows, :], ACT.Square, accum_out=yst[0:rows, 0:1]).then_inc(y_rstd, 1)
                act.wait_ge(y_rstd, 3 * i + 1)
                A(yst[0:rows, 1:2], yst[0:rows, 0:1], ACT.Ln, scale=1.0 / D, bias=epst[0:rows, :]).then_inc(y_rstd, 1)
                act.wait_ge(y_rstd, 3 * i + 2)
                A(yst[0:rows, 2:3], yst[0:rows, 1:2], ACT.Exp, scale=-0.5).then_inc(y_rstd, 1)

            act.wait_ge(const_in, 16 * 9)
            run(act, {"norm": norm, "proj": proj, "prep": prep, "decay": decay, "state": state, "tok": tok,
                      "query": query, "first": first, "step": step, "y_sum": y_sum_})

        @block.vector
        def _(dve):
            V = nc.vector

            def norm(g, k):
                n = N[g]
                dve.wait_ge(sq_done[g][k], DC + 2)
                dst = xn2 if k else mix
                for c in range(DC):
                    V.scalar_tensor_tensor(out=dst[:, c, 0:n], in0=hT[:, c, 0:n], scalar=nw[k][:, c:c + 1],
                                           in1=rst[:, 0:n], op0=ALU.mult, op1=ALU.mult).then_inc(xn_done[g][k], 1)

            def prep(g):
                n, L, w = N[g], PAD + N[g], slice(PAD, PAD + N[g])
                u = z[:, SP_]
                ps, cnt = pool_step[g], [0]

                def did(ins, wait=True):
                    ins.then_inc(ps, 1)
                    cnt[0] += 1
                    if wait:
                        dve.wait_ge(ps, cnt[0])

                if g == 0:
                    V.tensor_tensor(lbt[:, 8:12], lg[:, 0:4], lg[:, 4:8], ALU.subtract).then_inc(lb_diff, 1)
                dve.wait_ge(z_free[g], 2 + B_IN)
                if g == 0:
                    did(V.memset(u[:, :, 1:PAD], 0.0), False)
                    did(V.tensor_copy(u[:, :, PAD + SAMP0 - HIST:PAD + SAMP0], cache[:]), False)
                    did(V.tensor_copy(carry[:], u[:, :, PAD + META + P - HIST:PAD + META + P]), False)
                    did(V.tensor_copy(cs_buf[:], u[:, :, L - HIST:L]))
                else:
                    did(V.tensor_copy(u[:, :, 1:PAD], carry[:]), False)
                    did(V.tensor_copy(cp_buf[:], u[:, :, L - HIST:L]))
                a, b = bufs
                did(V.tensor_tensor(a[:, :, 2:L], u[:, :, 2:L], u[:, :, 1:L - 1], ALU.add))
                did(V.tensor_tensor(b[:, 1:4, 4:L], a[:, 1:4, 4:L], a[:, 1:4, 2:L - 2], ALU.add))
                did(V.tensor_tensor(a[:, 2:4, 8:L], b[:, 2:4, 8:L], b[:, 2:4, 4:L - 4], ALU.add))
                did(V.tensor_tensor(b[:, 3, 16:L], a[:, 3, 16:L], a[:, 3, 8:L - 8], ALU.add))
                if g == 0:
                    for i in range(4):
                        t = bufs[i % 2][:, i, PAD:PAD + META]
                        did(V.tensor_tensor(t, t, rcnt[:, i, :], ALU.mult), i == 3)
                for i in range(4):
                    t = bufs[i % 2][:, i, w]
                    did(V.scalar_tensor_tensor(out=t, in0=t, scalar=1.0 / WINDOWS[i], in1=u[:, i, w],
                                               op0=ALU.mult, op1=ALU.subtract), False)
                assert cnt[0] == PL[g]
                dp = dve_prep[g]
                tA = lev[:, 0:4 * n].rearrange("p (h c) -> p h c", h=4)
                tB = lev[:, 4 * n:8 * n].rearrange("p (h c) -> p h c", h=4)
                tC = mix[:, 0:4, 0:n]
                dve.wait_ge(ps, PL[g])
                dve.wait_ge(act_prep[g], 1)
                V.scalar_tensor_tensor(out=z[:, SQ, :, w], in0=z[:, SQ, :, w], scalar=float(P) ** -0.5, in1=tC,
                                       op0=ALU.mult, op1=ALU.mult).then_inc(dp, 1)
                dve.wait_ge(act_prep[g], 3)
                dve.wait_ge(lb_set, 2)
                for h in range(4):
                    V.tensor_scalar(z[:, SP_, h, w], tB[:, h, :], oml[:, h:h + 1], None, ALU.mult).then_inc(dp, 1)
                dve.wait_ge(act_prep[g], 4)
                for h in range(4):
                    V.scalar_tensor_tensor(out=z[:, SG, h, w], in0=tB[:, h, :], scalar=onorm[:, h:h + 1],
                                           in1=z[:, SG, h, w], op0=ALU.mult, op1=ALU.mult).then_inc(dp, 1)
                dve.wait_ge(act_prep[g], 8)
                for _, c0, T, _, _ in [c for c in CHUNKS if c[0] == g]:
                    for h in range(4):
                        V.tensor_tensor_scan(out=z[:, SF, h, PAD + c0:PAD + c0 + T], data0=ones[:, 0:T],
                                             data1=tA[:, h, c0:c0 + T], initial=0.0, op0=ALU.mult,
                                             op1=ALU.add).then_inc(dp, 1)

            def decay(ci):
                g, c0, T, nl, _ = CHUNKS[ci]
                cs = slice(PAD + c0, PAD + c0 + T)
                q, b, k_ = z[:, SQ, :, cs], z[:, SF, :, cs], z[:, SP_, :, cs]
                v4 = lambda t: t[:, 0:4 * T].rearrange("p (h t) -> p h t", h=4)
                le = count_before(n_lexp, ci)
                scans = DP_G + n_scans(g)
                dve.wait_ge(dve_prep[g], scans)

                def halves(l):
                    hw = 1 << l
                    f = lambda x: x.rearrange("p h (n two w) -> p h n two w", two=2, w=hw)
                    lv = f(v4(lev[:, l * 4 * T:(l + 1) * 4 * T]))
                    ref = f(b)[:, :, :, 0, hw - 1:hw].broadcast_to([P, 4, T // (2 * hw), hw])
                    return f, lv, ref

                for l in range(nl):
                    f, lv, ref = halves(l)
                    V.tensor_tensor(lv[:, :, :, 1, :], f(b)[:, :, :, 1, :], ref, ALU.subtract).then_inc(lsub, 1)
                    V.tensor_tensor(lv[:, :, :, 0, :], ref, f(b)[:, :, :, 0, :], ALU.subtract).then_inc(lsub, 1)
                if nl:
                    dve.wait_ge(lexp, le + 1)
                    V.tensor_tensor(v4(eb), v4(eb), q, ALU.mult).then_inc(lmul, 1)
                e0 = le + 5 + (1 if nl else 0)
                dve.wait_ge(lexp, e0)
                V.tensor_tensor(v4(ek), v4(ek), k_, ALU.mult).then_inc(lmul, 1)
                for l in range(nl):
                    f, lv, _ = halves(l)
                    dve.wait_ge(lexp, e0 + l + 1)
                    V.tensor_tensor(lv[:, :, :, 1, :], lv[:, :, :, 1, :], f(q)[:, :, :, 1, :], ALU.mult).then_inc(lmul, 1)
                    V.tensor_tensor(lv[:, :, :, 0, :], lv[:, :, :, 0, :], f(k_)[:, :, :, 0, :], ALU.mult).then_inc(lmul, 1)

            def heads(ci, hs):
                _, _, T, nl, _ = CHUNKS[ci]
                at = count_before(n_at, ci)
                if nl:
                    for h in hs:
                        ps = (P23 if h % 2 == 0 else P01)
                        m = msk[h % 2].rearrange("p (l t) -> p l t", l=8)[0:T, 0:nl + 1, 0:T]
                        dve.wait_ge(lmm, count_before(n_lmm, ci) + h + 1)
                        V.tensor_tensor(m, ps[0:T, :].rearrange("p (l t) -> p l t", l=8)[:, 0:nl + 1, 0:T],
                                        mask[0:T, 0:nl + 1, 0:T], ALU.mult).then_inc(at_done, 1)
                        dve.wait_ge(at_done, at + 2 * h + 1)
                        if h >= 2:
                            dve.wait_ge(o_mm, count_before(n_lmm, ci) + h - 1)
                        V.tensor_reduce(AT[h % 2][0:T, 0:T], m.rearrange("p l t -> p t l"), AX_X,
                                        ALU.add).then_inc(at_done, 1)

            def state(ci):
                g, c0, T, nl, stream = CHUNKS[ci]
                v4 = lambda t: t[:, 0:4 * T].rearrange("p (h t) -> p h t", h=4)
                G = z[:, SG, :, PAD + c0:PAD + c0 + T]
                S = Sp if stream == "p" else Ss
                dve.wait_ge(s_mm, count_before(n_smm, ci) + 1)
                if ci == 0:
                    V.tensor_copy(S[:].rearrange("p h v -> p (h v)"), b5[:]).then_inc(s_done, 1)
                else:
                    for h in range(4):
                        V.scalar_tensor_tensor(out=S[:, h, :], in0=S[:, h, :], scalar=dec[:, h:h + 1],
                                               in1=b5[:, h * P:(h + 1) * P], op0=ALU.mult, op1=ALU.add).then_inc(s_done, 1)
                if nl:
                    dve.wait_ge(on_done, count_before(n_on, ci) + 3)
                    V.tensor_tensor(ors[:, 0:4 * T], ors[:, 0:4 * T], b4[:, 0:4 * T], ALU.mult).then_inc(mo_done, 1)
                    dve.wait_ge(mo_done, count_before(n_mo, ci) + 1)
                    V.tensor_tensor(mix[:, 0:4, c0:c0 + T], v4(ors), G, ALU.mult).then_inc(mo_done, 1)

            def w_out(g, k, r):
                n = N[g]
                if k is None:
                    dve.sem_inc(h_free[g], 2)
                    return
                dve.wait_ge(blocks_done, k * WSLOTS + (g * B_ALL + B_IN + r + 1))
                h = hTf[:, bass.ds(k * (WSLOTS * NMAX) + r * NMAX, n)]
                V.tensor_tensor(h, h, P01[:, r % 2 * 512:r % 2 * 512 + n], ALU.add).then_inc(h_free[g], 1)

            def choose(s, s0):
                par = s0 % 2
                base = s * TK
                n = [0]

                def did(ins):
                    ins.then_inc(topk, 1)
                    n[0] += 1
                    return n[0]

                def need(v):
                    dve.wait_ge(topk, base + v)
                    own(dve)

                dve.wait_ge(staged, s + 1)
                st = stg[:, par]
                if s0 >= 1:
                    dve.wait_ge(topk, base)
                own(dve)
                for a in range(2):
                    did(V.max(sv[:, a, 0:8], st[:, a, :]))
                for a in range(2):
                    need(1 + a)
                    did(V.max_index(si[:, a, 0:8], sv[:, a, 0:8], st[:, a, :]))
                for a in range(2):
                    did(V.match_replace(rest[:, a, :], sv[:, a, 0:8], st[:, a, :], NEG))
                for a in range(2):
                    need(5 + a)
                    did(V.max(sv[:, a, 8:16], rest[:, a, :]))
                for a in range(2):
                    need(7 + a)
                    did(V.max_index(si[:, a, 8:16], sv[:, a, 8:16], rest[:, a, :]))
                c3 = cand[:].rearrange("p (i j) -> p i j", i=TOPK)
                did(V.tensor_tensor(c3, sv[:, 0, :].unsqueeze(2).broadcast_to([P, TOPK, TOPK]),
                                    sv[:, 1, :].unsqueeze(1).broadcast_to([P, TOPK, TOPK]), ALU.add))
                if s0 >= 2:
                    dve.wait_ge(exp_done, (s - 1) * 2)
                need(11)
                did(V.max(top[:, par, 0:8], cand[:]))
                need(12)
                did(V.match_replace(rest[:].rearrange("p a n -> p (a n)"), top[:, par, 0:8], cand[:], NEG))
                did(V.max_index(pos[:, 0:8], top[:, par, 0:8], cand[:]))
                need(13)
                did(V.max(top[:, par, 8:16], rest[:].rearrange("p a n -> p (a n)")))
                need(15)
                did(V.max_index(pos[:, 8:16], top[:, par, 8:16], rest[:].rearrange("p a n -> p (a n)")))
                need(16)
                did(V.tensor_scalar(hilo[:, 0, :], pos[:], 4, None, ALU.logical_shift_right))
                did(V.tensor_scalar(hilo[:, 1, :], pos[:], 15, None, ALU.bitwise_and))
                need(18)
                did(V.tensor_tensor(onehot[:], hilo[:].unsqueeze(3).broadcast_to([P, 2, TOPK, TOPK]),
                                    iota16.unsqueeze(1).unsqueeze(1).broadcast_to([P, 2, TOPK, TOPK]),
                                    ALU.is_equal))
                need(19)
                did(V.tensor_tensor(onehot[:], onehot[:], si[:].unsqueeze(2).broadcast_to([P, 2, TOPK, TOPK]),
                                    ALU.mult))
                need(20)
                did(V.tensor_reduce(ab[:], onehot[:], AX_X, ALU.add))
                need(21)
                if s0 >= 2:
                    dve.wait_ge(idx_copied, s - 1)
                did(V.scalar_tensor_tensor(out=idxU[:, par, :], in0=ab[:, 0, :], scalar=float(NKEYS), in1=ab[:, 1, :],
                                           op0=ALU.mult, op1=ALU.add))
                assert n[0] == TK

            def first(s):
                choose(s, s)

            def step(s, s0, quarter, do_u, do_v, nxt):
                if do_v and quarter == 0:
                    par = 1 - s0 % 2
                    dve.wait_ge(exp_done, s * 2)
                    V.reciprocal(exs[:, par, 2:3], exs[:, par, 1:2]).then_inc(w_done, 1)
                    dve.wait_ge(w_done, s * 2 - 1)
                    dve.wait_ge(gelu_done, s)
                    V.scalar_tensor_tensor(out=wgt[:, par, :], in0=ge[:, par, :], scalar=exs[:, par, 2:3],
                                           in1=ex[:, par, :], op0=ALU.mult, op1=ALU.mult).then_inc(w_done, 1)
                if nxt and quarter == 0:
                    choose(s + 1, s0 + 1)
                if do_u:
                    x = xtok[TILES[tile_of(s0)][0]]
                    for j in range(4 * quarter, 4 * quarter + 4):
                        dve.wait_ge(u_in[j % RU], s * 32 + 16 * (j // RU + 1))
                        V.tensor_tensor_reduce(out=Ur[:, j % RU, :], in0=Ur[:, j % RU, :], in1=x, scale=1.0, scalar=0.0,
                                               op0=ALU.mult, op1=ALU.add,
                                               accum_out=adot[:, s0 % 2, j:j + 1]).then_inc(u_free, 1)
                if do_v and TILES[tile_of(s0 - 1)][0] != "pk":
                    j, h = 4 * quarter + 3, htok[TILES[tile_of(s0 - 1)][0]]
                    dve.wait_ge(v_in[3], (s - 1) * 64 + 16 * (quarter + 1))
                    dve.wait_ge(v3_free, (s - 1) * 4 + quarter + 1)
                    dve.wait_ge(w_done, s * 2)
                    V.scalar_tensor_tensor(out=h, in0=Vr[:, 3, :], scalar=wgt[:, 1 - s0 % 2, j:j + 1], in1=h,
                                           op0=ALU.mult, op1=ALU.add).then_inc(v3_free, 1)

            def y_sum_(i):
                name = TILES[i][0]
                rows = SAMP if name == "pk" else P
                dve.wait_ge(acc_close, i + 1)
                dve.wait_ge(v3_free, 4 * (TILES[i][1] + TILES[i][2]) + 1)
                for k, acc in enumerate((b6, b7)):
                    h = htok[name][0:rows, k * 512:(k + 1) * 512]
                    V.tensor_tensor(h, h, acc[0:rows, :], ALU.add).then_inc(y_sum, 1)

            def y_out(i):
                name = TILES[i][0]
                rows = SAMP if name == "pk" else P
                dve.wait_ge(y_rstd, 3 * i + 3)
                h = htok[name][0:rows, :]
                V.scalar_tensor_tensor(out=h, in0=h, scalar=yst[0:rows, 2:3], in1=nf[0:rows, :],
                                       op0=ALU.mult, op1=ALU.mult).then_inc(y_done, 1)

            dve.wait_ge(const_in, 16 * 9)
            dve.wait_ge(const_set, 3)
            dve.sem_inc(u_free, RU)
            run(dve, {"norm": norm, "prep": prep, "decay": decay, "heads01": lambda c: heads(c, (0, 1)),
                      "heads23": lambda c: heads(c, (2, 3)), "state": state, "w_out": w_out, "first": first, "step": step,
                      "y_sum": y_sum_, "y_out": y_out})

        @block.tensor
        def _(pe):
            M = nc.tensor.matmul

            def norm(g, k):
                n = N[g]
                for c in range(DC):
                    pe.wait_ge(sq_done[g][k], c + 1)
                    M(P23[:, 512:512 + n], ones[:], sqb[c % 2][:, 0:n], start=(c == 0),
                      stop=(c == DC - 1)).then_inc(ss_done[g][k], 1)

            def block_of(g, k, B0, r, src, free):
                n = N[g]
                pe.wait_ge(w_in[r], k * 16 + 16 * ((g * B_ALL + B0) // WSLOTS + 1))
                pe.wait_ge(free, k * WSLOTS + (r + 1))
                for c in range(DC):
                    last = M(P01[:, r % 2 * 512:r % 2 * 512 + n], wring[:, r, c * P:(c + 1) * P], src[:, c, 0:n],
                             start=(c == 0), stop=(c == DC - 1))
                last.then_inc(blocks_done, 1)

            def proj(g, k, r):
                if k is None:
                    pe.wait_ge(xn_done[g][0], DC)
                else:
                    block_of(g, k, 0, r, mix, z_free[g])

            def prep(g):
                n, w = N[g], slice(PAD, PAD + N[g])
                pe.wait_ge(pool_step[g], PL[g])
                for i in range(4):
                    if i >= 2:
                        pe.wait_ge(pool_out[g], i - 1)
                    M(P23[:, i % 2 * 512:i % 2 * 512 + n], pw[:, i, :], bufs[i % 2][:, i, w], start=True,
                      stop=True).then_inc(pool_mm[g], 1)

            def decay(ci):
                g, c0, T, nl, _ = CHUNKS[ci]
                if ci:
                    pe.wait_ge(mo_done, count_before(n_mo, ci))
                    pe.wait_ge(s_done, count_before(n_sd, ci))
                for h in range(4):
                    last = nc.tensor.transpose(b4[0:T, h * P:(h + 1) * P], z[:, SI, h, PAD + c0:PAD + c0 + T], ident[:])
                last.then_inc(ctr, 1)
                pe.wait_ge(lmul, count_before(n_lmul, ci) + 1 + (1 if nl else 0))
                for h in range(4):
                    last = nc.tensor.transpose(b5[0:T, h * P:(h + 1) * P], ek[:, h * T:(h + 1) * T], ident[:])
                last.then_inc(ctr, 1)

            def levels(ci, h):
                g, c0, T, nl, _ = CHUNKS[ci]
                cs = slice(PAD + c0, PAD + c0 + T)
                ps = (P23 if h % 2 == 0 else P01)
                if h == 0:
                    pe.wait_ge(lmul, count_before(n_lmul, ci + 1))
                if h >= 2:
                    pe.wait_ge(at_done, count_before(n_at, ci) + 2 * (h - 2) + 1)
                M(ps[0:T, 0:T], z[:, SP_, h, cs], z[:, SQ, h, cs], start=True, stop=True)
                for l in range(nl):
                    m = lev[:, (l * 4 + h) * T:(l * 4 + h + 1) * T]
                    last = M(ps[0:T, (l + 1) * P:(l + 1) * P + T], m, m, start=True, stop=True)
                last.then_inc(lmm, 1)

            def outputs(ci, h):
                _, _, T, _, stream = CHUNKS[ci]
                S = Sp if stream == "p" else Ss
                pe.wait_ge(at_done, count_before(n_at, ci) + 2 * h + 2)
                o = b4[:, h * T:(h + 1) * T]
                M(o, vtok[0:T, h * P:(h + 1) * P], AT[h % 2][0:T, 0:T], start=True, stop=False)
                M(o, S[:, h, :], eb[:, h * T:(h + 1) * T], start=False, stop=True).then_inc(o_mm, 1)

            def heads01(ci):
                if CHUNKS[ci][3]:
                    levels(ci, 0)
                    levels(ci, 1)
                    pe.wait_ge(ctr_out, count_before(n_ctr, ci) + 1)
                    outputs(ci, 0)

            def heads23(ci):
                if CHUNKS[ci][3]:
                    levels(ci, 2)
                    outputs(ci, 1)
                    levels(ci, 3)
                    outputs(ci, 2)
                    outputs(ci, 3)

            def state(ci):
                _, _, T, nl, _ = CHUNKS[ci]
                pe.wait_ge(ctr_out, count_before(n_ctr, ci) + 2)
                for h in range(4):
                    last = M(b5[:, h * P:(h + 1) * P], ktok[0:T, h * P:(h + 1) * P], vtok[0:T, h * P:(h + 1) * P],
                             start=True, stop=True)
                last.then_inc(s_mm, 1)
                if nl:
                    pe.wait_ge(on_done, count_before(n_on, ci) + 1)
                    M(P23[:, 0:4 * T], ones[:], osq[:, 0:4 * T], start=True, stop=True).then_inc(osum_done, 1)

            def w_out(g, k, r):
                if k is None:
                    pe.wait_ge(mo_done, count_before(n_mo, 3 if g == 0 else 6))
                    pe.wait_ge(pool_out[g], 4)
                else:
                    block_of(g, k, B_IN, r, mix, h_free[g])

            def tok(g, u):
                is_x, (name, c0), half = tok_unit(g, u)
                if is_x and u == n_tr[g] // 2:
                    pe.wait_ge(xn_done[g][1], DC)
                if u >= 2:
                    pe.wait_ge(tr_out[g], u - 1)
                for c in range(4):
                    dst = TB[u % 2][:, c * P:(c + 1) * P]
                    blk = (xn2 if is_x else hT)[:, half * 4 + c, c0:c0 + (SAMP if name == "pk" else P)]
                    if name != "pk":
                        last = nc.tensor.transpose(dst, blk, ident[:])
                    elif not is_x:
                        last = nc.tensor.transpose(dst[0:SAMP, :], blk, ident[:])
                    else:
                        for q in range(4):
                            last = M(dst[SAMP * q:SAMP * (q + 1), :], blk, ident[:], start=True, stop=True)
                last.then_inc(tr_mm[g], 1)

            def query(g, k, r):
                if k is None:
                    return
                j = 4 * k + r
                if j < B_Q:
                    block_of(g, k, B_IN + B_OUT, r, xn2, q_free[g])
                if not j:
                    return
                r = (j - 1) % 4
                pe.wait_ge(q_free[g], 2 + j)
                pe.wait_ge(sc_free[g], j)
                o = r % 2 * 512
                for i, (name, c0) in enumerate(group_tiles[g]):
                    if name == "pk":
                        last = M(P23[SAMP * r:SAMP * (r + 1), o + i * P:o + (i + 1) * P], qT[r % 2][:, c0:c0 + SAMP],
                                 wring[:, r, D:WQ], start=True, stop=True)
                    else:
                        last = M(P23[:, o + i * P:o + (i + 1) * P], qT[r % 2][:, c0:c0 + P], wring[:, r, D:WQ],
                                 start=True, stop=True)
                last.then_inc(sc_mm[g], 1)

            def step(s, s0, quarter, do_u, do_v, nxt):
                if not do_v:
                    return
                i = tile_of(s0 - 1)
                name, t0, tn = TILES[i]
                m = SAMP if name == "pk" else P
                if s0 - 1 == t0 and quarter == 0:
                    if i:
                        pe.wait_ge(y_sum, 2 * i)
                    for acc in (b6, b7):
                        M(acc[0:m, :], zb[0:1, 0:m], zb[0:1, :], start=True, stop=False)
                for r in range(4 if name == "pk" else 3):
                    pe.wait_ge(v_in[r], (s - 1) * 64 + 16 * (quarter + 1))
                    if r < 3:
                        pe.wait_ge(diag_done, (s - 1) * 12 + 3 * quarter + r + 1)
                    else:
                        pe.wait_ge(diag3_done, (s0 - 1 - t0) * 4 + quarter + 1)
                    for k, acc in enumerate((b6, b7)):
                        last = M(acc[0:m, :], diag[:, r, 0:m], Vr[:, r, k * 512:(k + 1) * 512], start=False,
                                 stop=False)
                    last.then_inc(v_free if r < 3 else v3_free, 1)
                if s0 == t0 + tn and quarter == 3:
                    for acc in (b6, b7):
                        last = M(acc[0:m, :], zb[0:1, 0:m], zb[0:1, :], start=False, stop=True)
                    last.then_inc(acc_close, 1)

            pe.wait_ge(const_in, 16 * 9)
            pe.wait_ge(const_set, 3)
            pe.sem_inc(v_free, 3)
            pe.sem_inc(v3_free, 1)
            run(pe, {"norm": norm, "proj": proj, "prep": prep, "decay": decay, "heads01": heads01,
                     "heads23": heads23, "state": state, "w_out": w_out, "tok": tok,
                     "query": query, "step": step})


def kernel(**inputs):
    import numpy as np
    import concourse.bacc as bacc
    from concourse.bass_utils import run_bass_kernel_spmd

    a = {k: np.asarray(v) for k, v in inputs.items()}
    f32 = np.float32
    blocks = lambda w: w.reshape(DC, P, -1)
    x = a["x_prompt"][0]
    xcols = np.concatenate([a["meta_tokens"], x[:P], np.zeros((GAP, D), f32), a["x_sample"][0], x[P:]], axis=0)
    xT = xcols.T.reshape(DC, P, COLS).transpose(1, 0, 2)

    def weight_blocks(w):
        return w.reshape(DC, P, -1, P).transpose(2, 1, 0, 3).reshape(-1, P, DC * P)

    w_io = np.concatenate([weight_blocks(a["w_in"][0]), weight_blocks(a["w_out"][0])], axis=0)
    order = [(2 * r + (k >> 1)) * 2 + (k & 1) for k in range(4) for r in range(4)]
    subk = a["peer_subkeys"][0].reshape(B_Q, NKEYS, P).transpose(0, 2, 1)
    w_q = np.concatenate([weight_blocks(a["peer_w_query"][0])[order], subk[order]], axis=2)
    fm = lambda v: v.reshape(-1, P).T
    lg = a["hgrn_lb_logits"]
    vecs = np.concatenate([fm(a["norm_mix"][0]), fm(a["norm_ffn"][0]), fm(a["hgrn_out_norm"][0]),
                           fm(a["pool_scale"][0]), fm(lg[0]), fm(lg[1])], axis=1)
    t = np.arange(P)
    masks = np.zeros((P, 8, P), f32)
    masks[:, 0, :] = t[:, None] == t[None, :]
    for l in range(7):
        same = (t[:, None] >> (l + 1)) == (t[None, :] >> (l + 1))
        masks[:, l + 1, :] = same & ((t[:, None] >> l) % 2 == 0) & ((t[None, :] >> l) % 2 == 1)
    small = np.zeros((P, 80), f32)
    small[:, 0:16] = np.arange(16)
    for i, w in enumerate(WINDOWS):
        small[:, 16 + 16 * i:32 + 16 * i] = w / np.minimum(w, np.arange(META) + 1.0)
    arrays = {
        "xT": xT, "w_io": w_io, "w_q": w_q, "pool_w": a["pool_w"][0].transpose(1, 0, 2), "vecs": vecs, "masks": masks,
        "ident": np.eye(P, dtype=f32), "sel": np.tile(np.eye(SAMP, dtype=f32), (4, 1)), "small": small,
        "cacheT": a["cache_pool"][0, 0].T.reshape(4, P, HIST).transpose(1, 0, 2),
        "state": a["state_hgrn"][0, 0].transpose(1, 0, 2), "nf": a["norm_final"],
        "peer_u": a["peer_u"][0], "peer_v": a["peer_v"][0],
    }
    arrays = {k: np.ascontiguousarray(v) for k, v in arrays.items()}
    outs = {"y_prompt": (SEQ, D), "y_sample": (SAMP, D), "sp": (P, 4, P), "ss": (P, 4, P), "cp": (P, 4, HIST),
            "cs": (P, 4, HIST)}
    nc = bacc.Bacc("TRN2", target_bir_lowering=False, num_devices=1)
    args = [nc.dram_tensor("in_" + k, v.shape, FP32, kind="ExternalInput").ap() for k, v in arrays.items()]
    args += [nc.dram_tensor("out_" + k, s, FP32, kind="ExternalOutput").ap() for k, s in outs.items()]
    build(nc, *args)
    r = run_bass_kernel_spmd(nc, [{"in_" + k: v for k, v in arrays.items()}], core_ids=[0]).results[0]
    o = {k: r["out_" + k] for k in outs}
    st = lambda s: s.transpose(1, 0, 2)[None, None]
    hist = lambda c: c.transpose(2, 1, 0).reshape(HIST, 4 * P)[None, None]
    return (o["y_prompt"][None], o["y_sample"][None], st(o["sp"]), hist(o["cp"]), st(o["ss"]), hist(o["cs"]))
```

```python
import concourse.bass as bass
from concourse import mybir
from contextlib import ExitStack

FP32 = mybir.dt.float32
BF16 = mybir.dt.bfloat16
U32 = mybir.dt.uint32
ALU = mybir.AluOpType
ACT = mybir.ActivationFunctionType
AX_X = mybir.AxisListType.X

P = 128
D = 1024
DC = D // P
SEQ, META, SAMP = 512, 16, 32
H_A = 4
HIST = 15
WINDOWS = (2, 4, 8, 16)
PEER_H, TOPK, NKEYS = 8, 16, 128
EPS = 1e-6
NEG = -3.0e38

GAP = 16
N = (META + P + GAP + SAMP, SEQ - P)
COLS = sum(N)
SAMP0 = META + P + GAP
NMAX = max(N)
PAD = 16
ZW = NMAX + PAD
CHUNKS = [(0, 0, META, 0, "p"), (0, META, P, 7, "p"), (0, SAMP0, SAMP, 5, "s"),
          (1, 0, P, 7, "p"), (1, P, P, 7, "p"), (1, 2 * P, P, 7, "p")]

B_IN, B_OUT, B_Q = 20, 8, 16
B_ALL = B_IN + B_OUT + B_Q
WSLOTS = 4
WQ = D + NKEYS

TILES = [("t0", 0, 8), ("pk", 8, 2), ("t1", 10, 8), ("t2", 18, 8), ("t3", 26, 8)]
STEPS = 34
G0_STEPS = 10
RU, RV = 8, 4
BY_DVE = (3,)
T_GATHER, T_ROW_PE, T_ROW_DVE, T_DOT, T_CHOOSE, SLACK = 5.95, 1.75, 1.2, 1.2, 8.0, 14.0
T_PART = {"norm": (7, 4), "proj": (5.1, 0), "pool_sum": (0, 9), "pool_mm": (2.6, 0), "decay_in": (0, 5),
          "keys": (0, 3), "decay": (0.5, 5), "decay_mul": (0, 6), "heads01": (4.5, 4.5), "heads23": (5, 4.5), "state": (2, 3),
          "w_out": (5.1, 0.5), "tok": (0.6, 0), "query": (5.8, 0)}


def count_before(per_chunk, chunk):
    return sum(per_chunk(c) for c in CHUNKS[:chunk])


def build(nc, xT, w_io, w_q, pool_w, vecs, masks, ident_d, sel_d, small_d, cacheT, state_d, nf_d, peer_u, peer_v,
          y_prompt, y_sample, sp_out, ss_out, cp_out, cs_out):
    ctx = ExitStack()
    with ctx:
        def sb(name, shape, dt=FP32):
            return ctx.enter_context(nc.sbuf_tensor(name, shape, dt))

        def sem(name):
            return ctx.enter_context(nc.semaphore(name))

        hT = sb("hT", [P, DC, NMAX])
        mix = sb("mix", [P, DC, NMAX])
        S_FLOATS = G0_STEPS * 2 * NKEYS
        arena = sb("arena", [P, S_FLOATS + 20 * ZW])
        lev = sb("lev", [P, 7 * 4 * P])
        wring = sb("wring", [P, WSLOTS, WQ])
        mask = sb("mask", [P, 8, P])
        nf = sb("nf", [P, D])
        ident = sb("ident", [P, P])
        sel = sb("sel", [P, SAMP])
        ones = sb("ones", [P, P])
        small = sb("small", [P, 16 + 4 * 16])
        pw = sb("pw", [P, 4, P])
        vec = sb("vec", [P, 40])
        lbt = sb("lbt", [P, 12])
        epst = sb("epst", [P, 1])
        cache = sb("cache", [P, 4, HIST])
        carry = sb("carry", [P, 4, HIST])
        cs_buf = sb("cs_buf", [P, 4, HIST])
        cp_buf = sb("cp_buf", [P, 4, HIST])
        Sp = sb("Sp", [P, 4, P])
        Ss = sb("Ss", [P, 4, P])
        htok0 = sb("htok0", [P, D])
        htoks = sb("htoks", [SAMP, D])
        xtok0 = sb("xtok0", [P, D])
        xtokp = sb("xtokp", [P, D])
        Ur = sb("Ur", [P, RU, D])
        Vr = sb("Vr", [P, RV, D])
        ctmp = sb("ctmp", [P, 2 * 8 * P + 2 * P + 4 * 4 * P])
        dec = sb("dec", [P, 4])
        stg = sb("stg", [P, 2, 2, NKEYS])
        rest = sb("rest", [P, 2, NKEYS])
        cand = sb("cand", [P, TOPK * TOPK])
        onehot = sb("onehot", [P, 2, TOPK, TOPK])
        sv = sb("sv", [P, 2, TOPK])
        si = sb("si", [P, 2, TOPK], U32)
        top = sb("top", [P, 2, TOPK])
        pos = sb("pos", [P, TOPK], U32)
        hilo = sb("hilo", [P, 2, TOPK], U32)
        ab = sb("ab", [P, 2, TOPK])
        idxU = sb("idxU", [P, 2, TOPK], U32)
        idxV = sb("idxV", [P, 2, TOPK], U32)
        ex = sb("ex", [P, 2, TOPK])
        exs = sb("exs", [P, 2, 4])
        adot = sb("adot", [P, 2, TOPK])
        ge = sb("ge", [P, 2, TOPK])
        wgt = sb("wgt", [P, 2, TOPK])
        diag = sb("diag", [P, RV, P])
        ydump = sb("ydump", [P, D], BF16)
        yst = sb("yst", [P, 4])
        zb = sb("zb", [1, 512], BF16)

        nw = (vec[:, 0:8], vec[:, 8:16])
        onorm, pscale, lg = vec[:, 16:20], vec[:, 20:24], vec[:, 24:32]
        lb, oml = lbt[:, 0:4], lbt[:, 4:8]
        iota16, rcnt = small[:, 0:16], small[:, 16:80].rearrange("p (g t) -> p g t", g=4)
        zf_ = arena[:, S_FLOATS:S_FLOATS + 20 * ZW]
        z = zf_.rearrange("p (s h c) -> p s h c", s=5, h=4)
        SP_, SQ, SF, SG, SI = range(5)
        bufs = [lev[:, 0:4 * ZW].rearrange("p (g c) -> p g c", g=4),
                lev[:, 4 * ZW:8 * ZW].rearrange("p (g c) -> p g c", g=4)]
        xn2 = lev[:, 0:DC * NMAX].rearrange("p (c n) -> p c n", c=DC)
        msk = [ctmp[:, i * 1024:(i + 1) * 1024] for i in range(2)]
        AT = [ctmp[:, 2048 + i * P:2048 + (i + 1) * P] for i in range(2)]
        o4 = 2048 + 2 * P
        eb, ek, vtok, ktok = [ctmp[:, o4 + i * 512:o4 + (i + 1) * 512] for i in range(4)]
        osq, ors = [msk[0][:, i * 512:(i + 1) * 512] for i in range(2)]
        sqb = [ctmp[:, i * NMAX:(i + 1) * NMAX] for i in range(2)]
        rst = ctmp[:, 2 * NMAX:3 * NMAX]
        qT = [ctmp[:, (3 + i) * NMAX:(4 + i) * NMAX] for i in range(2)]
        htok = {"t0": htok0[:], "pk": htoks[:]}
        xtok = {"t0": xtok0[:], "pk": xtokp[:]}
        mixf, hTf = mix[:].rearrange("p c n -> p (c n)"), hT[:].rearrange("p c n -> p (c n)")
        for i in range(3):
            htok[f"t{i + 1}"] = mixf[:, i * D:(i + 1) * D]
            xtok[f"t{i + 1}"] = hTf[:, i * D:(i + 1) * D]

        P01 = ctx.enter_context(nc.psum_tensor("P01", [P, 1024], FP32))
        P23 = ctx.enter_context(nc.psum_tensor("P23", [P, 1024], FP32))
        b4, b5, b6, b7 = [ctx.enter_context(nc.psum_tensor(f"b{i}", [P, 512], FP32)) for i in (4, 5, 6, 7)]
        TB = (b4, b5)

        x_in = [sem(f"x_in{g}") for g in range(2)]
        const_in, const_set, late_in = sem("const_in"), sem("const_set"), sem("late_in")
        w_in = [sem(f"w_in{r}") for r in range(WSLOTS)]
        blocks_done = sem("blocks_done")
        lb_diff, lb_set = sem("lb_diff"), sem("lb_set")
        sq_done = [[sem(f"sq_done{g}{k}") for k in range(2)] for g in range(2)]
        ss_done = [[sem(f"ss_done{g}{k}") for k in range(2)] for g in range(2)]
        xn_done = [[sem(f"xn_done{g}{k}") for k in range(2)] for g in range(2)]
        z_free = [sem(f"z_free{g}") for g in range(2)]
        h_free = [sem(f"h_free{g}") for g in range(2)]
        q_free = [sem(f"q_free{g}") for g in range(2)]
        pool_step = [sem(f"pool_step{g}") for g in range(2)]
        pool_mm = [sem(f"pool_mm{g}") for g in range(2)]
        pool_out = [sem(f"pool_out{g}") for g in range(2)]
        act_prep = [sem(f"act_prep{g}") for g in range(2)]
        dve_prep = [sem(f"dve_prep{g}") for g in range(2)]
        lsub, lexp, lmul, ctr, ctr_out, lmm, at_done, o_mm, s_mm, s_done, on_done, osum_done, mo_done = [
            sem(n) for n in ("lsub", "lexp", "lmul", "ctr", "ctr_out", "lmm", "at_done", "o_mm", "s_mm", "s_done",
                             "on_done", "osum_done", "mo_done")]
        tr_mm = [sem(f"tr_mm{g}") for g in range(2)]
        tr_out = [sem(f"tr_out{g}") for g in range(2)]
        sc_mm = [sem(f"sc_mm{g}") for g in range(2)]
        sc_free = [sem(f"sc_free{g}") for g in range(2)]
        staged, topk, exp_done, gelu_done, w_done = [sem(n) for n in (
            "staged", "topk", "exp_done", "gelu_done", "w_done")]
        diag_done = [sem(f"diag_done{r}") for r in range(RV)]
        idx_copied = sem("idx_copied")
        u_free = sem("u_free")
        v_free = [sem(f"v_free{r}") for r in range(RV)]
        u_in = [sem(f"u_in{r}") for r in range(RU)]
        v_in = [sem(f"v_in{r}") for r in range(RV)]
        acc_open, acc_close, y_sum, y_rstd, y_done, stored = [sem(n) for n in (
            "acc_open", "acc_close", "y_sum", "y_rstd", "y_done", "stored")]

        full = lambda c: 1 if c[3] else 0
        n_lsub = lambda c: 2 * c[3]
        n_lexp = lambda c: 5 + full(c) + c[3]
        n_lmul = lambda c: 1 + full(c) + 2 * c[3]
        n_ctr = lambda c: 2
        n_lmm = lambda c: 4 * full(c)
        n_at = lambda c: 8 * full(c)
        n_smm = lambda c: 1
        n_sd = lambda c: 1 if not full(c) else 4
        n_on = lambda c: 3 * full(c)
        n_os = lambda c: full(c)
        n_mo = lambda c: 2 * full(c)
        PL = ((16, 10))
        n_scans = lambda g: 4 * sum(1 for c in CHUNKS if c[0] == g)
        n_prep = lambda g: n_scans(g) + 8
        group_tiles = ((("t0", META), ("pk", SAMP0)), (("t1", 0), ("t2", P), ("t3", 2 * P)))
        n_tr = (8, 12)
        TK = 22

        waited = {n: sem(f"waited_{n}") for n in ("vector", "gpsimd")}

        def tok_unit(g, u):
            per = 2 * len(group_tiles[g])
            return u >= per, group_tiles[g][u % per // 2], u % 2

        def own(eng):
            eng.sem_inc(waited["gpsimd" if eng is nc.gpsimd else "vector"], 1)

        def trunk(g):
            after = {5: "pool_sum", 7: "pool_mm", 12: "decay_in", 19: "keys"}
            parts = [("norm", g, 0)]
            for j in range(B_IN):
                parts.append(("proj", g, j))
                if j in after:
                    parts.append((after[j], g))
            for c in range(len(CHUNKS)):
                if CHUNKS[c][0] == g:
                    parts += [(n, c) for n in ("decay", "decay_mul", "heads01", "heads23", "state")]
            parts += [("w_out", g, j) for j in range(B_OUT)] + [("norm", g, 1)]
            parts += [("tok", g, u) for u in range(n_tr[g])] + [("query", g, j) for j in range(B_Q + 1)]
            return parts

        def tile_of(s):
            return [i for i, t in enumerate(TILES) if t[1] <= s < t[1] + t[2]][0]

        by_dve = {}

        def slots_of(s, quarter):
            return () if TILES[tile_of(s)][0] == "pk" else by_dve.get((s, quarter), BY_DVE)

        def diags_before(r, s, quarter):
            return sum(r not in slots_of(v, q) for v in range(s + 1) for q in range(4) if (v, q) < (s, quarter))

        def summed_before(s, quarter, r=0):
            rows = [(v, q, x) for v in range(max(s - 4, 0), s + 1) for q in range(4) for x in slots_of(v, q)
                    if (v, q, x) < (s, quarter, r)]
            return (rows[-1][2], 4 * rows[-1][0] + rows[-1][1] + 2) if rows else None

        def steps(last, between):
            between, out = list(between), [("first", 0)]
            left = {4: len(between) - B_Q // 2, G0_STEPS: B_Q // 2, G0_STEPS + 4: 0}
            ends = {t[1] + t[2]: i for i, t in enumerate(TILES)}
            dma = pe = dve = 0.0
            s = 0
            while s <= last:
                go, rows, nxt = s < last, s > 0, s + 1 < last
                while len(between) > left.get(s + 1, len(between)):
                    pe += T_PART[between[0][0]][0]
                    dma = max(dma, pe)
                    out.append(between.pop(0))
                for quarter in range(4):
                    out.append(("step", s, s, quarter, go, rows, nxt))
                    dma += T_GATHER * (go + rows)
                    dve += 4 * T_DOT * go + (T_CHOOSE if nxt and quarter == 0 else 0)
                    if rows:
                        if between and TILES[tile_of(s - 1)][0] != "pk":
                            n = min(range(5), key=lambda n: max(pe + (4 - n) * T_ROW_PE, dve + n * T_ROW_DVE))
                            by_dve[s - 1, quarter] = tuple(range(RV - n, RV))
                        n = len(slots_of(s - 1, quarter))
                        pe += (4 - n) * T_ROW_PE
                        dve += n * T_ROW_DVE
                    while between:
                        t_pe, t_dve = T_PART[between[0][0]]
                        if between[0][:2] == ("query", 0):
                            t_pe *= N[0] / N[1]
                        if max(pe + t_pe, dve + t_dve) > dma + SLACK:
                            break
                        pe, dve = pe + t_pe, dve + t_dve
                        out.append(between.pop(0))
                    pe, dve = max(pe, dma - T_GATHER * 2), max(dve, dma - T_GATHER * 2)
                if s in ends:
                    out.append(("y_sum", ends[s]))
                if s - 1 in ends:
                    out.append(("y_out", ends[s - 1]))
                s += 1
                in_tile = [t for t in TILES if t[1] < s < t[1] + t[2]]
                if not between and in_tile and s == in_tile[0][1] + 2 and s > G0_STEPS:
                    pairs = 2 if in_tile[0][1] + 8 == last else 3
                    out.append(("loop", s, pairs))
                    s += 2 * pairs
            return out + [("y_out", ends[last])]

        early = len(trunk(0)) - B_Q // 2
        plan = trunk(0)[:early] + steps(STEPS, trunk(0)[early:] + trunk(1))

        def run(eng, parts, loops=()):
            mine = [p for p in plan if p[0] in parts or p[0] == "loop"]
            i = 0
            while i < len(mine):
                kind, *a = mine[i]
                n = 0
                while i + n < len(mine) and mine[i + n][0] == kind and mine[i + n][1] == a[0]:
                    n += 1
                if kind == "loop":
                    s0, pairs = a
                    if "step" in parts:
                        with eng.Fori(0, pairs) as k:
                            for par in range(2):
                                for quarter in range(4):
                                    parts["step"](k * 2 + (s0 + par), s0 + par, quarter, True, True, True)
                elif kind in ("proj", "w_out", "query"):
                    g, j = a
                    if j == 0:
                        parts[kind](g, None, 0)
                    if kind in loops and j % 4 == 0 and n >= 8:
                        with eng.Fori(j // 4, j // 4 + n // 4) as k:
                            for r in range(4):
                                parts[kind](g, k, r)
                        i += n // 4 * 4 - 1
                    else:
                        parts[kind](g, j // 4, j % 4)
                else:
                    parts[kind](*a)
                i += 1

        block = ctx.enter_context(nc.Block())

        def ysteps(sp, a, b):
            for i in range(a, b):
                name = TILES[i][0]
                sp.wait_ge(y_done, i + 1)
                if name == "pk":
                    sp.dma_start(y_sample, htok[name]).then_inc(stored, 16)
                else:
                    n = int(name[1])
                    sp.dma_start(y_prompt[n * P:(n + 1) * P, :], htok[name]).then_inc(stored, 16)

        @block.sync
        def _(sp):
            sp.dma_start(hT[:, :, 0:N[0]], xT[:, :, 0:N[0]]).then_inc(x_in[0], 16)
            sp.dma_start(vec[:, 0:32], vecs).then_inc(const_in, 16)

            def load(B, r, query):
                if query:
                    sp.dma_start(wring[:, r, :], w_q[bass.ds(B, 1), :, :].rearrange("b p m -> p (b m)")
                                 ).then_inc(w_in[r], 16)
                else:
                    sp.dma_start(wring[:, r, 0:D], w_io[bass.ds(B, 1), :, :].rearrange("b p m -> p (b m)")
                                 ).then_inc(w_in[r], 16)

            for g in range(2):
                base = g * B_ALL
                if g:
                    sp.wait_ge(tr_out[0], n_tr[0])
                    sp.wait_ge(xn_done[0][1], DC)
                    sp.dma_start(hT[:, :, 0:N[1]], xT[:, :, N[0]:COLS]).then_inc(x_in[1], 16)
                for r in range(WSLOTS):
                    if g:
                        sp.wait_ge(blocks_done, base + r - 1)
                    load(r, r, False)
                if g == 0:
                    for dst, src in ((cache[:], cacheT), (small[:], small_d), (pw[:], pool_w), (ident[:], ident_d),
                                     (mask[:], masks), (Ss[:], state_d), (sel[:], sel_d),
                                     (nf[:], nf_d.partition_broadcast(P))):
                        sp.dma_start(dst, src).then_inc(late_in, 16)
                with sp.Fori(1, (B_IN + B_OUT) // WSLOTS) as k:
                    for r in range(WSLOTS):
                        sp.wait_ge(blocks_done, k * WSLOTS + (base + r + 1 - WSLOTS))
                        load(k * WSLOTS + r, r, False)
                for r in range(WSLOTS):
                    sp.wait_ge(blocks_done, base + B_IN + B_OUT + r + 1 - WSLOTS)
                    load(r, r, True)
                with sp.Fori(1, B_Q // WSLOTS) as k:
                    for r in range(WSLOTS):
                        sp.wait_ge(blocks_done, k * WSLOTS + (base + B_IN + B_OUT + r - 1))
                        load(k * WSLOTS + r, r, True)
            sp.wait_ge(pool_step[1], 2)
            sp.dma_start(cs_out, cs_buf[:]).then_inc(stored, 16)
            sp.dma_start(cp_out, cp_buf[:]).then_inc(stored, 16)
            sp.wait_ge(s_done, count_before(n_sd, 6))
            sp.dma_start(ss_out, Ss[:]).then_inc(stored, 16)
            sp.dma_start(sp_out, Sp[:]).then_inc(stored, 16)
            ysteps(sp, 0, 5)
            sp.wait_ge(stored, 16 * 9)

        @block.gpsimd
        def _(pool):
            nc.gpsimd.memset(ones[:], 1.0).then_inc(const_set, 1)
            nc.gpsimd.memset(epst[:], EPS).then_inc(const_set, 1)
            nc.gpsimd.memset(zb[:], 0.0).then_inc(const_set, 1)

            def step(s, s0, quarter, do_u, do_v, _next):
                par = s0 % 2
                if do_u and quarter == 0:
                    pool.wait_ge(topk, s * TK + TK)
                    own(pool)
                for r in range(4):
                    j = 4 * quarter + r
                    if do_u:
                        pool.wait_ge(u_free, s * TOPK + j + 1)
                        own(pool)
                        pool.indirect_dma_start(Ur[:, j % RU, :], None, peer_u, bass.IndirectOffsetOnAxis(
                            ap=idxU[:, par, j:j + 1], axis=0)).then_inc(u_in[j % RU], 16)
                    if do_v:
                        if j == 0:
                            pool.wait_ge(idx_copied, s)
                        pool.wait_ge(v_free[r], (s - 1) * 4 + (quarter + 1))
                        own(pool)
                        pool.indirect_dma_start(Vr[:, r, :], None, peer_v, bass.IndirectOffsetOnAxis(
                            ap=idxV[:, 1 - par, j:j + 1], axis=0)).then_inc(v_in[r], 16)
                if do_u and quarter == 3:
                    nc.gpsimd.tensor_copy(idxV[:, par, :], idxU[:, par, :]).then_inc(idx_copied, 1)

            run(pool, {"step": step})

        @block.scalar
        def _(act):
            A = nc.scalar.activation

            def norm(g, k):
                n = N[g]
                if k == 0:
                    act.wait_ge(x_in[g], 16)
                    act.wait_ge(const_set, 2)
                else:
                    act.wait_ge(h_free[g], 2 + DC)
                for c in range(DC):
                    if c >= 2:
                        act.wait_ge(ss_done[g][k], c - 1)
                    A(sqb[c % 2][:, 0:n], hT[:, c, 0:n], ACT.Square).then_inc(sq_done[g][k], 1)
                act.wait_ge(ss_done[g][k], DC)
                A(rst[:, 0:n], P23[:, 512:512 + n], ACT.Ln, scale=1.0 / D, bias=epst[:]).then_inc(sq_done[g][k], 1)
                act.wait_ge(sq_done[g][k], DC + 1)
                A(rst[:, 0:n], rst[:, 0:n], ACT.Exp, scale=-0.5).then_inc(sq_done[g][k], 1)

            def proj(g, k, r):
                if k is None:
                    act.sem_inc(z_free[g], 2)
                    return
                act.wait_ge(blocks_done, g * B_ALL + 4 * k + r + 1)
                A(z[:, k, r, PAD:PAD + N[g]], P01[:, r % 2 * 512:r % 2 * 512 + N[g]],
                  ACT.Silu if k in (SQ, SG) else ACT.Copy).then_inc(z_free[g], 1)

            def pool_mm_(g):
                n = N[g]
                act.wait_ge(const_in, 16)
                act.wait_ge(late_in, 16 * 8)
                for i in range(4):
                    act.wait_ge(pool_mm[g], i + 1)
                    A(z[:, SP_, i, PAD:PAD + n], P23[:, i % 2 * 512:i % 2 * 512 + n], ACT.Copy,
                      scale=pscale[:, i:i + 1]).then_inc(pool_out[g], 1)

            def decay_in(g):
                n, w = N[g], slice(PAD, PAD + N[g])
                tA = lev[:, 0:4 * n].rearrange("p (h c) -> p h c", h=4)
                tB = lev[:, 4 * n:8 * n].rearrange("p (h c) -> p h c", h=4)
                if g == 0:
                    act.wait_ge(lb_diff, 1)
                    A(lb, lbt[:, 8:12], ACT.Sigmoid).then_inc(lb_set, 1)
                    A(oml, lbt[:, 8:12], ACT.Sigmoid, scale=-1.0).then_inc(lb_set, 1)
                act.wait_ge(z_free[g], 2 + 4 * (SF + 1))
                A(tA, z[:, SF, :, w], ACT.Sigmoid).then_inc(act_prep[g], 1)
                A(tB, z[:, SF, :, w], ACT.Sigmoid, scale=-1.0).then_inc(act_prep[g], 1)
                act.wait_ge(act_prep[g], 1)
                act.wait_ge(lb_set, 2)
                for h in range(4):
                    A(tA[:, h, :], tA[:, h, :], ACT.Ln, scale=oml[:, h:h + 1], bias=lb[:, h:h + 1]).then_inc(act_prep[g], 1)

            def decay(ci):
                g, c0, T, nl, _ = c = CHUNKS[ci]
                b = z[:, SF, :, PAD + c0:PAD + c0 + T]
                last = b[:, :, T - 1]
                v4 = lambda t: t[:, 0:4 * T].rearrange("p (h t) -> p h t", h=4)
                scans = 4 * (1 + sum(1 for x in CHUNKS[:ci] if x[0] == g))
                if ci:
                    act.wait_ge(s_mm, count_before(n_smm, ci))
                act.wait_ge(ctr, count_before(n_ctr, ci) + 1)
                A(vtok[0:T, :], b4[0:T, :], ACT.Copy).then_inc(ctr_out, 1)
                act.wait_ge(dve_prep[g], scans)
                if nl:
                    A(v4(eb), b, ACT.Exp).then_inc(lexp, 1)
                for h in range(4):
                    A(ek[:, h * T:(h + 1) * T], b[:, h, :], ACT.Exp, scale=-1.0, bias=last[:, h:h + 1]).then_inc(lexp, 1)
                A(dec[:], last, ACT.Exp).then_inc(lexp, 1)
                for l in range(nl):
                    act.wait_ge(lsub, count_before(n_lsub, ci) + 2 * l + 2)
                    lv = lev[:, l * 4 * T:(l + 1) * 4 * T]
                    A(lv, lv, ACT.Exp).then_inc(lexp, 1)

            def heads01(ci):
                T = CHUNKS[ci][2]
                act.wait_ge(ctr, count_before(n_ctr, ci) + 2)
                A(ktok[0:T, :], b5[0:T, :], ACT.Copy).then_inc(ctr_out, 1)

            def state(ci):
                g, c0, T, nl, _ = CHUNKS[ci]
                if nl:
                    act.wait_ge(o_mm, count_before(n_lmm, ci) + 4)
                    A(osq[:, 0:4 * T], b4[:, 0:4 * T], ACT.Square).then_inc(on_done, 1)
                    act.wait_ge(osum_done, count_before(n_os, ci) + 1)
                    A(ors[:, 0:4 * T], P23[:, 0:4 * T], ACT.Ln, scale=1.0 / P ** 2, bias=epst[:]).then_inc(on_done, 1)
                    act.wait_ge(on_done, count_before(n_on, ci) + 2)
                    A(ors[:, 0:4 * T], ors[:, 0:4 * T], ACT.Exp, scale=-0.5).then_inc(on_done, 1)

            def tok(g, u):
                is_x, (name, _), half = tok_unit(g, u)
                rows = SAMP if (name == "pk" and not is_x) else P
                act.wait_ge(tr_mm[g], u + 1)
                A((xtok if is_x else htok)[name][0:rows, half * 512:(half + 1) * 512], TB[u % 2][0:rows, :],
                  ACT.Copy).then_inc(tr_out[g], 1)

            def query(g, k, r):
                n = N[g]
                if k is None:
                    act.sem_inc(q_free[g], 2)
                    act.sem_inc(sc_free[g], 2)
                    return
                j = 4 * k + r
                if j < B_Q:
                    act.wait_ge(blocks_done, g * B_ALL + B_IN + B_OUT + j + 1)
                    A(qT[r % 2][:, 0:n], P01[:, r % 2 * 512:r % 2 * 512 + n], ACT.Copy).then_inc(q_free[g], 1)
                if not j:
                    return
                k, r = divmod(j - 1, 4)
                act.wait_ge(sc_mm[g], j)
                o = r % 2 * 512
                at = k // 2 * 1024 + r * 256 + k % 2 * NKEYS
                if g:
                    dst = arena[:, S_FLOATS:S_FLOATS + 3 * 2048].rearrange("p (t s) -> p t s", t=3)
                    A(dst[:, :, at:at + NKEYS], P23[:, o:o + 384].rearrange("p (t s) -> p t s", t=3),
                      ACT.Copy).then_inc(sc_free[g], 1)
                else:
                    A(arena[:, at:at + NKEYS], P23[:, o:o + P], ACT.Copy)
                    q, at = slice(SAMP * r, SAMP * (r + 1)), k * NKEYS + 8 * 256
                    A(arena[q, at:at + NKEYS], P23[q, o + P:o + 2 * P], ACT.Copy).then_inc(sc_free[g], 1)

            def stage(s, s0):
                g = s0 >= G0_STEPS
                act.wait_ge(sc_free[g], 2 + (B_Q // 2 if s0 - g * G0_STEPS < 4 else B_Q))
                if s0 >= 2:
                    act.wait_ge(topk, (s - 1) * TK)
                A(stg[:, s0 % 2].rearrange("p a n -> p (a n)"), arena[:, bass.ds(s * 256, 256)], ACT.Copy).then_inc(staged, 1)

            def exps(s, s0):
                par = s0 % 2
                act.wait_ge(topk, s * TK + 16)
                if s0 >= 2:
                    act.wait_ge(w_done, (s - 1) * 2)
                A(exs[:, par, 0:1], top[:, par, 0:1], ACT.Copy, scale=-1.0).then_inc(exp_done, 1)
                act.wait_ge(exp_done, s * 2 + 1)
                A(ex[:, par, :], top[:, par, :], ACT.Exp, bias=exs[:, par, 0:1],
                  accum_out=exs[:, par, 1:2]).then_inc(exp_done, 1)

            def first(s):
                stage(s, s)
                exps(s, s)

            def step(s, s0, quarter, do_u, do_v, nxt):
                if nxt and quarter == 0:
                    stage(s + 1, s0 + 1)
                if do_v:
                    par = 1 - s0 % 2
                    if quarter == 0:
                        act.wait_ge(u_free, s * TOPK + RU)
                        A(ge[:, par, :], adot[:, par, :], ACT.Gelu).then_inc(gelu_done, 1)
                        act.wait_ge(w_done, s * 2)
                    packed = TILES[tile_of(s0 - 1)][0] == "pk"
                    for qd in {0: (0, 1), 1: (2,), 2: (3,), 3: ()}[quarter]:
                        for r in range(RV):
                            if r in slots_of(s0 - 1, qd):
                                continue
                            j = 4 * qd + r
                            act.wait_ge(v_free[r], (s - 1) * 4 + (qd + 1))
                            src = sel if packed else ident
                            A(diag[:, r, 0:SAMP if packed else P], src[:], ACT.Copy,
                              scale=wgt[:, par, j:j + 1]).then_inc(diag_done[r], 1)
                if nxt and quarter == 3:
                    exps(s + 1, s0 + 1)

            def y_sum_(i):
                name = TILES[i][0]
                rows = SAMP if name == "pk" else P
                act.wait_ge(y_sum, 2 * (i + 1))
                A(ydump[0:rows, :], htok[name][0:rows, :], ACT.Square, accum_out=yst[0:rows, 0:1]).then_inc(y_rstd, 1)
                act.wait_ge(y_rstd, 3 * i + 1)
                A(yst[0:rows, 1:2], yst[0:rows, 0:1], ACT.Ln, scale=1.0 / D, bias=epst[0:rows, :]).then_inc(y_rstd, 1)
                act.wait_ge(y_rstd, 3 * i + 2)
                A(yst[0:rows, 2:3], yst[0:rows, 1:2], ACT.Exp, scale=-0.5).then_inc(y_rstd, 1)

            run(act, {"norm": norm, "proj": proj, "pool_mm": pool_mm_, "decay_in": decay_in, "decay": decay, "heads01": heads01, "state": state, "tok": tok,
                      "query": query, "first": first, "step": step, "y_sum": y_sum_})

        @block.vector
        def _(dve):
            V = nc.vector

            def norm(g, k):
                n = N[g]
                dve.wait_ge(sq_done[g][k], DC + 2)
                dst = xn2 if k else mix
                for c in range(DC):
                    V.scalar_tensor_tensor(out=dst[:, c, 0:n], in0=hT[:, c, 0:n], scalar=nw[k][:, c:c + 1],
                                           in1=rst[:, 0:n], op0=ALU.mult, op1=ALU.mult).then_inc(xn_done[g][k], 1)

            def pool_sum(g):
                n, L, w = N[g], PAD + N[g], slice(PAD, PAD + N[g])
                u = z[:, SP_]
                ps, cnt = pool_step[g], [0]

                def did(ins, wait=True):
                    ins.then_inc(ps, 1)
                    cnt[0] += 1
                    if wait:
                        dve.wait_ge(ps, cnt[0])

                dve.wait_ge(late_in, 16 * 8)
                dve.wait_ge(z_free[g], 2 + 4)
                if g == 0:
                    did(V.memset(u[:, :, 1:PAD], 0.0), False)
                    did(V.tensor_copy(u[:, :, PAD + SAMP0 - HIST:PAD + SAMP0], cache[:]), False)
                    did(V.tensor_copy(carry[:], u[:, :, PAD + META + P - HIST:PAD + META + P]), False)
                    did(V.tensor_copy(cs_buf[:], u[:, :, L - HIST:L]))
                else:
                    did(V.tensor_copy(u[:, :, 1:PAD], carry[:]), False)
                    did(V.tensor_copy(cp_buf[:], u[:, :, L - HIST:L]))
                a, b = bufs
                did(V.tensor_tensor(a[:, :, 2:L], u[:, :, 2:L], u[:, :, 1:L - 1], ALU.add))
                did(V.tensor_tensor(b[:, 1:4, 4:L], a[:, 1:4, 4:L], a[:, 1:4, 2:L - 2], ALU.add))
                did(V.tensor_tensor(a[:, 2:4, 8:L], b[:, 2:4, 8:L], b[:, 2:4, 4:L - 4], ALU.add))
                did(V.tensor_tensor(b[:, 3, 16:L], a[:, 3, 16:L], a[:, 3, 8:L - 8], ALU.add))
                if g == 0:
                    for i in range(4):
                        t = bufs[i % 2][:, i, PAD:PAD + META]
                        did(V.tensor_tensor(t, t, rcnt[:, i, :], ALU.mult), i == 3)
                for i in range(4):
                    t = bufs[i % 2][:, i, w]
                    did(V.scalar_tensor_tensor(out=t, in0=t, scalar=1.0 / WINDOWS[i], in1=u[:, i, w],
                                               op0=ALU.mult, op1=ALU.subtract), False)
                assert cnt[0] == PL[g]

            def decay_in(g):
                n = N[g]
                tA = lev[:, 0:4 * n].rearrange("p (h c) -> p h c", h=4)
                dve.wait_ge(act_prep[g], 6)
                for _, c0, T, _, _ in [c for c in CHUNKS if c[0] == g]:
                    for h in range(4):
                        V.tensor_tensor_scan(out=z[:, SF, h, PAD + c0:PAD + c0 + T], data0=ones[:, 0:T],
                                             data1=tA[:, h, c0:c0 + T], initial=0.0, op0=ALU.mult,
                                             op1=ALU.add).then_inc(dve_prep[g], 1)

            def keys(g):
                n, w = N[g], slice(PAD, PAD + N[g])
                tB = lev[:, 4 * n:8 * n].rearrange("p (h c) -> p h c", h=4)
                dve.wait_ge(z_free[g], 2 + 4 * (SG + 1))
                for h in range(4):
                    V.tensor_scalar(z[:, SG, h, w], z[:, SG, h, w], onorm[:, h:h + 1], float(P) ** -0.5, ALU.mult,
                                    ALU.mult).then_inc(dve_prep[g], 1)
                dve.wait_ge(blocks_done, g * B_ALL + B_IN)
                for h in range(4):
                    V.tensor_scalar(mix[:, h, 0:n], tB[:, h, :], oml[:, h:h + 1], None, ALU.mult).then_inc(dve_prep[g], 1)

            def halves(l, T):
                hw = 1 << l
                f = lambda x: x.rearrange("p h (n two w) -> p h n two w", two=2, w=hw)
                return f, f(lev[:, l * 4 * T:(l + 1) * 4 * T].rearrange("p (h t) -> p h t", h=4)), hw

            def decay(ci):
                g, c0, T, nl, _ = CHUNKS[ci]
                cs = slice(PAD + c0, PAD + c0 + T)
                b = z[:, SF, :, cs]
                dve.wait_ge(dve_prep[g], n_prep(g))
                for l in range(nl):
                    f, lv, hw = halves(l, T)
                    ref = f(b)[:, :, :, 0, hw - 1:hw].broadcast_to([P, 4, T // (2 * hw), hw])
                    V.tensor_tensor(lv[:, :, :, 1, :], f(b)[:, :, :, 1, :], ref, ALU.subtract).then_inc(lsub, 1)
                    V.tensor_tensor(lv[:, :, :, 0, :], ref, f(b)[:, :, :, 0, :], ALU.subtract).then_inc(lsub, 1)

            def decay_mul(ci):
                g, c0, T, nl, _ = CHUNKS[ci]
                q, k_ = z[:, SQ, :, PAD + c0:PAD + c0 + T], mix[:, 0:4, c0:c0 + T]
                v4 = lambda t: t[:, 0:4 * T].rearrange("p (h t) -> p h t", h=4)
                le = count_before(n_lexp, ci)
                if nl:
                    dve.wait_ge(lexp, le + 1)
                    V.tensor_tensor(v4(eb), v4(eb), q, ALU.mult).then_inc(lmul, 1)
                e0 = le + 5 + (1 if nl else 0)
                dve.wait_ge(lexp, e0)
                V.tensor_tensor(v4(ek), v4(ek), k_, ALU.mult).then_inc(lmul, 1)
                for l in range(nl):
                    f, lv, _ = halves(l, T)
                    dve.wait_ge(lexp, e0 + l + 1)
                    V.tensor_tensor(lv[:, :, :, 1, :], lv[:, :, :, 1, :], f(q)[:, :, :, 1, :], ALU.mult).then_inc(lmul, 1)
                    V.tensor_tensor(lv[:, :, :, 0, :], lv[:, :, :, 0, :], f(k_)[:, :, :, 0, :], ALU.mult).then_inc(lmul, 1)

            def heads(ci, hs):
                _, _, T, nl, _ = CHUNKS[ci]
                at = count_before(n_at, ci)
                if nl:
                    for h in hs:
                        ps = (P23 if h % 2 == 0 else P01)
                        m = msk[h % 2].rearrange("p (l t) -> p l t", l=8)[0:T, 0:nl + 1, 0:T]
                        dve.wait_ge(lmm, count_before(n_lmm, ci) + h + 1)
                        V.tensor_tensor(m, ps[0:T, :].rearrange("p (l t) -> p l t", l=8)[:, 0:nl + 1, 0:T],
                                        mask[0:T, 0:nl + 1, 0:T], ALU.mult).then_inc(at_done, 1)
                        dve.wait_ge(at_done, at + 2 * h + 1)
                        if h >= 2:
                            dve.wait_ge(o_mm, count_before(n_lmm, ci) + h - 1)
                        V.tensor_reduce(AT[h % 2][0:T, 0:T], m.rearrange("p l t -> p t l"), AX_X,
                                        ALU.add).then_inc(at_done, 1)

            def state(ci):
                g, c0, T, nl, stream = CHUNKS[ci]
                v4 = lambda t: t[:, 0:4 * T].rearrange("p (h t) -> p h t", h=4)
                G = z[:, SG, :, PAD + c0:PAD + c0 + T]
                S = Sp if stream == "p" else Ss
                dve.wait_ge(s_mm, count_before(n_smm, ci) + 1)
                if ci == 0:
                    V.tensor_copy(S[:].rearrange("p h v -> p (h v)"), b5[:]).then_inc(s_done, 1)
                else:
                    for h in range(4):
                        V.scalar_tensor_tensor(out=S[:, h, :], in0=S[:, h, :], scalar=dec[:, h:h + 1],
                                               in1=b5[:, h * P:(h + 1) * P], op0=ALU.mult, op1=ALU.add).then_inc(s_done, 1)
                if nl:
                    dve.wait_ge(on_done, count_before(n_on, ci) + 3)
                    V.tensor_tensor(ors[:, 0:4 * T], ors[:, 0:4 * T], b4[:, 0:4 * T], ALU.mult).then_inc(mo_done, 1)
                    dve.wait_ge(mo_done, count_before(n_mo, ci) + 1)
                    V.tensor_tensor(mix[:, 0:4, c0:c0 + T], v4(ors), G, ALU.mult).then_inc(mo_done, 1)

            def w_out(g, k, r):
                n = N[g]
                if k is None:
                    dve.sem_inc(h_free[g], 2)
                    return
                dve.wait_ge(blocks_done, k * WSLOTS + (g * B_ALL + B_IN + r + 1))
                h = hTf[:, bass.ds(k * (WSLOTS * NMAX) + r * NMAX, n)]
                V.tensor_tensor(h, h, P01[:, r % 2 * 512:r % 2 * 512 + n], ALU.add).then_inc(h_free[g], 1)

            def choose(s, s0):
                par = s0 % 2
                base = s * TK
                n = [0]

                def did(ins):
                    ins.then_inc(topk, 1)
                    n[0] += 1
                    return n[0]

                def need(v):
                    dve.wait_ge(topk, base + v)
                    own(dve)

                dve.wait_ge(staged, s + 1)
                st = stg[:, par]
                if s0 >= 1:
                    dve.wait_ge(topk, base)
                own(dve)
                for a in range(2):
                    did(V.max(sv[:, a, 0:8], st[:, a, :]))
                for a in range(2):
                    need(1 + a)
                    did(V.max_index(si[:, a, 0:8], sv[:, a, 0:8], st[:, a, :]))
                for a in range(2):
                    did(V.match_replace(rest[:, a, :], sv[:, a, 0:8], st[:, a, :], NEG))
                for a in range(2):
                    need(5 + a)
                    did(V.max(sv[:, a, 8:16], rest[:, a, :]))
                for a in range(2):
                    need(7 + a)
                    did(V.max_index(si[:, a, 8:16], sv[:, a, 8:16], rest[:, a, :]))
                c3 = cand[:].rearrange("p (i j) -> p i j", i=TOPK)
                did(V.tensor_tensor(c3, sv[:, 0, :].unsqueeze(2).broadcast_to([P, TOPK, TOPK]),
                                    sv[:, 1, :].unsqueeze(1).broadcast_to([P, TOPK, TOPK]), ALU.add))
                if s0 >= 2:
                    dve.wait_ge(exp_done, (s - 1) * 2)
                need(11)
                did(V.max(top[:, par, 0:8], cand[:]))
                need(12)
                did(V.match_replace(rest[:].rearrange("p a n -> p (a n)"), top[:, par, 0:8], cand[:], NEG))
                did(V.max_index(pos[:, 0:8], top[:, par, 0:8], cand[:]))
                need(13)
                did(V.max(top[:, par, 8:16], rest[:].rearrange("p a n -> p (a n)")))
                need(15)
                did(V.max_index(pos[:, 8:16], top[:, par, 8:16], rest[:].rearrange("p a n -> p (a n)")))
                need(16)
                did(V.tensor_scalar(hilo[:, 0, :], pos[:], 4, None, ALU.logical_shift_right))
                did(V.tensor_scalar(hilo[:, 1, :], pos[:], 15, None, ALU.bitwise_and))
                need(18)
                did(V.tensor_tensor(onehot[:], hilo[:].unsqueeze(3).broadcast_to([P, 2, TOPK, TOPK]),
                                    iota16.unsqueeze(1).unsqueeze(1).broadcast_to([P, 2, TOPK, TOPK]),
                                    ALU.is_equal))
                need(19)
                did(V.tensor_tensor(onehot[:], onehot[:], si[:].unsqueeze(2).broadcast_to([P, 2, TOPK, TOPK]),
                                    ALU.mult))
                need(20)
                did(V.tensor_reduce(ab[:], onehot[:], AX_X, ALU.add))
                need(21)
                if s0 >= 2:
                    dve.wait_ge(idx_copied, s - 1)
                did(V.scalar_tensor_tensor(out=idxU[:, par, :], in0=ab[:, 0, :], scalar=float(NKEYS), in1=ab[:, 1, :],
                                           op0=ALU.mult, op1=ALU.add))
                assert n[0] == TK

            def first(s):
                choose(s, s)

            def step(s, s0, quarter, do_u, do_v, nxt):
                if do_v and quarter == 0:
                    par = 1 - s0 % 2
                    dve.wait_ge(exp_done, s * 2)
                    V.reciprocal(exs[:, par, 2:3], exs[:, par, 1:2]).then_inc(w_done, 1)
                    dve.wait_ge(w_done, s * 2 - 1)
                    dve.wait_ge(gelu_done, s)
                    V.scalar_tensor_tensor(out=wgt[:, par, :], in0=ge[:, par, :], scalar=exs[:, par, 2:3],
                                           in1=ex[:, par, :], op0=ALU.mult, op1=ALU.mult).then_inc(w_done, 1)
                if nxt and quarter == 0:
                    choose(s + 1, s0 + 1)
                if do_u:
                    x = xtok[TILES[tile_of(s0)][0]]
                    for j in range(4 * quarter, 4 * quarter + 4):
                        dve.wait_ge(u_in[j % RU], s * 32 + 16 * (j // RU + 1))
                        V.tensor_tensor_reduce(out=Ur[:, j % RU, :], in0=Ur[:, j % RU, :], in1=x, scale=1.0, scalar=0.0,
                                               op0=ALU.mult, op1=ALU.add,
                                               accum_out=adot[:, s0 % 2, j:j + 1]).then_inc(u_free, 1)
                if do_v:
                    for r in slots_of(s0 - 1, quarter):
                        j, h = 4 * quarter + r, htok[TILES[tile_of(s0 - 1)][0]]
                        dve.wait_ge(v_in[r], (s - 1) * 64 + 16 * (quarter + 1))
                        before = summed_before(s0 - 1, quarter, r)
                        if before:
                            dve.wait_ge(v_free[before[0]], s * 4 + (before[1] - 4 * s0))
                        dve.wait_ge(w_done, s * 2)
                        V.scalar_tensor_tensor(out=h, in0=Vr[:, r, :], scalar=wgt[:, 1 - s0 % 2, j:j + 1], in1=h,
                                               op0=ALU.mult, op1=ALU.add).then_inc(v_free[r], 1)

            def y_sum_(i):
                name = TILES[i][0]
                rows = SAMP if name == "pk" else P
                dve.wait_ge(acc_close, i + 1)
                r, v = summed_before(TILES[i][1] + TILES[i][2] - 1, 3, RV)
                dve.wait_ge(v_free[r], v)
                for k, acc in enumerate((b6, b7)):
                    h = htok[name][0:rows, k * 512:(k + 1) * 512]
                    V.tensor_tensor(h, h, acc[0:rows, :], ALU.add).then_inc(y_sum, 1)

            def y_out(i):
                name = TILES[i][0]
                rows = SAMP if name == "pk" else P
                dve.wait_ge(y_rstd, 3 * i + 3)
                h = htok[name][0:rows, :]
                V.scalar_tensor_tensor(out=h, in0=h, scalar=yst[0:rows, 2:3], in1=nf[0:rows, :],
                                       op0=ALU.mult, op1=ALU.mult).then_inc(y_done, 1)

            dve.wait_ge(const_in, 16)
            dve.wait_ge(const_set, 3)
            dve.sem_inc(u_free, RU)
            V.tensor_tensor(lbt[:, 8:12], lg[:, 0:4], lg[:, 4:8], ALU.subtract).then_inc(lb_diff, 1)
            run(dve, {"norm": norm, "pool_sum": pool_sum, "decay_in": decay_in, "keys": keys, "decay": decay, "decay_mul": decay_mul, "heads01": lambda c: heads(c, (0, 1)),
                      "heads23": lambda c: heads(c, (2, 3)), "state": state, "w_out": w_out, "first": first, "step": step,
                      "y_sum": y_sum_, "y_out": y_out}, ("w_out",))

        @block.tensor
        def _(pe):
            M = nc.tensor.matmul

            def norm(g, k):
                n = N[g]
                for c in range(DC):
                    pe.wait_ge(sq_done[g][k], c + 1)
                    M(P23[:, 512:512 + n], ones[:], sqb[c % 2][:, 0:n], start=(c == 0),
                      stop=(c == DC - 1)).then_inc(ss_done[g][k], 1)

            def block_of(g, k, B0, r, src, free):
                n = N[g]
                pe.wait_ge(w_in[r], k * 16 + 16 * ((g * B_ALL + B0) // WSLOTS + 1))
                pe.wait_ge(free, k * WSLOTS + (r + 1))
                for c in range(DC):
                    last = M(P01[:, r % 2 * 512:r % 2 * 512 + n], wring[:, r, c * P:(c + 1) * P], src(c),
                             start=(c == 0), stop=(c == DC - 1))
                last.then_inc(blocks_done, 1)

            def proj(g, k, r):
                if k is None:
                    pe.wait_ge(xn_done[g][0], DC)
                else:
                    block_of(g, k, 0, r, lambda c: mix[:, c, 0:N[g]], z_free[g])

            def pool_mm_(g):
                n, w = N[g], slice(PAD, PAD + N[g])
                pe.wait_ge(late_in, 16 * 8)
                pe.wait_ge(pool_step[g], PL[g])
                for i in range(4):
                    if i >= 2:
                        pe.wait_ge(pool_out[g], i - 1)
                    M(P23[:, i % 2 * 512:i % 2 * 512 + n], pw[:, i, :], bufs[i % 2][:, i, w], start=True,
                      stop=True).then_inc(pool_mm[g], 1)

            def decay(ci):
                g, c0, T, nl, _ = CHUNKS[ci]
                if ci:
                    pe.wait_ge(mo_done, count_before(n_mo, ci))
                pe.wait_ge(z_free[g], 2 + B_IN)
                for h in range(4):
                    last = nc.tensor.transpose(b4[0:T, h * P:(h + 1) * P], z[:, SI, h, PAD + c0:PAD + c0 + T], ident[:])
                last.then_inc(ctr, 1)

            def levels(ci, h):
                g, c0, T, nl, _ = CHUNKS[ci]
                cs = slice(PAD + c0, PAD + c0 + T)
                ps = (P23 if h % 2 == 0 else P01)
                if h == 0:
                    pe.wait_ge(lmul, count_before(n_lmul, ci + 1))
                if h >= 2:
                    pe.wait_ge(at_done, count_before(n_at, ci) + 2 * (h - 2) + 1)
                M(ps[0:T, 0:T], mix[:, h, c0:c0 + T], z[:, SQ, h, cs], start=True, stop=True)
                for l in range(nl):
                    m = lev[:, (l * 4 + h) * T:(l * 4 + h + 1) * T]
                    last = M(ps[0:T, (l + 1) * P:(l + 1) * P + T], m, m, start=True, stop=True)
                last.then_inc(lmm, 1)

            def outputs(ci, h):
                _, _, T, _, stream = CHUNKS[ci]
                S = Sp if stream == "p" else Ss
                pe.wait_ge(at_done, count_before(n_at, ci) + 2 * h + 2)
                o = b4[:, h * T:(h + 1) * T]
                M(o, vtok[0:T, h * P:(h + 1) * P], AT[h % 2][0:T, 0:T], start=True, stop=False)
                M(o, S[:, h, :], eb[:, h * T:(h + 1) * T], start=False, stop=True).then_inc(o_mm, 1)

            def heads01(ci):
                _, _, T, nl, _ = CHUNKS[ci]
                if nl:
                    levels(ci, 0)
                    levels(ci, 1)
                if ci:
                    pe.wait_ge(s_done, count_before(n_sd, ci))
                pe.wait_ge(lmul, count_before(n_lmul, ci) + 1 + (1 if nl else 0))
                for h in range(4):
                    last = nc.tensor.transpose(b5[0:T, h * P:(h + 1) * P], ek[:, h * T:(h + 1) * T], ident[:])
                last.then_inc(ctr, 1)

            def heads23(ci):
                if CHUNKS[ci][3]:
                    pe.wait_ge(ctr_out, count_before(n_ctr, ci) + 1)
                    outputs(ci, 0)
                    levels(ci, 2)
                    outputs(ci, 1)
                    levels(ci, 3)

            def state(ci):
                _, _, T, nl, _ = CHUNKS[ci]
                if nl:
                    outputs(ci, 2)
                    outputs(ci, 3)
                pe.wait_ge(ctr_out, count_before(n_ctr, ci) + 2)
                for h in range(4):
                    last = M(b5[:, h * P:(h + 1) * P], ktok[0:T, h * P:(h + 1) * P], vtok[0:T, h * P:(h + 1) * P],
                             start=True, stop=True)
                last.then_inc(s_mm, 1)
                if nl:
                    pe.wait_ge(on_done, count_before(n_on, ci) + 1)
                    M(P23[:, 0:4 * T], ones[:], osq[:, 0:4 * T], start=True, stop=True).then_inc(osum_done, 1)

            def w_out(g, k, r):
                if k is None:
                    pe.wait_ge(mo_done, count_before(n_mo, 3 if g == 0 else 6))
                    pe.wait_ge(pool_out[g], 4)
                else:
                    block_of(g, k, B_IN, r, lambda c: mix[:, c, 0:N[g]] if c < 4 else z[:, SP_, c - 4, PAD:PAD + N[g]],
                             h_free[g])

            def tok(g, u):
                is_x, (name, c0), half = tok_unit(g, u)
                if is_x and u == n_tr[g] // 2:
                    pe.wait_ge(xn_done[g][1], DC)
                if u >= 2:
                    pe.wait_ge(tr_out[g], u - 1)
                for c in range(4):
                    dst = TB[u % 2][:, c * P:(c + 1) * P]
                    blk = (xn2 if is_x else hT)[:, half * 4 + c, c0:c0 + (SAMP if name == "pk" else P)]
                    if name != "pk":
                        last = nc.tensor.transpose(dst, blk, ident[:])
                    elif not is_x:
                        last = nc.tensor.transpose(dst[0:SAMP, :], blk, ident[:])
                    else:
                        for q in range(4):
                            last = M(dst[SAMP * q:SAMP * (q + 1), :], blk, ident[:], start=True, stop=True)
                last.then_inc(tr_mm[g], 1)

            def query(g, k, r):
                if k is None:
                    return
                j = 4 * k + r
                if j < B_Q:
                    block_of(g, k, B_IN + B_OUT, r, lambda c: xn2[:, c, 0:N[g]], q_free[g])
                if not j:
                    return
                r = (j - 1) % 4
                pe.wait_ge(q_free[g], 2 + j)
                pe.wait_ge(sc_free[g], j)
                o = r % 2 * 512
                for i, (name, c0) in enumerate(group_tiles[g]):
                    if name == "pk":
                        last = M(P23[SAMP * r:SAMP * (r + 1), o + i * P:o + (i + 1) * P], qT[r % 2][:, c0:c0 + SAMP],
                                 wring[:, r, D:WQ], start=True, stop=True)
                    else:
                        last = M(P23[:, o + i * P:o + (i + 1) * P], qT[r % 2][:, c0:c0 + P], wring[:, r, D:WQ],
                                 start=True, stop=True)
                last.then_inc(sc_mm[g], 1)

            def step(s, s0, quarter, do_u, do_v, nxt):
                if not do_v:
                    return
                i = tile_of(s0 - 1)
                name, t0, tn = TILES[i]
                m = SAMP if name == "pk" else P
                if s0 - 1 == t0 and quarter == 0:
                    if i:
                        pe.wait_ge(y_sum, 2 * i)
                    for acc in (b6, b7):
                        M(acc[0:m, :], zb[0:1, 0:m], zb[0:1, :], start=True, stop=False)
                for r in range(RV):
                    if r in slots_of(s0 - 1, quarter):
                        continue
                    pe.wait_ge(v_in[r], (s - 1) * 64 + 16 * (quarter + 1))
                    pe.wait_ge(diag_done[r], s * 4 + (diags_before(r, s0 - 1, quarter) + 1 - 4 * s0))
                    for k, acc in enumerate((b6, b7)):
                        last = M(acc[0:m, :], diag[:, r, 0:m], Vr[:, r, k * 512:(k + 1) * 512], start=False,
                                 stop=False)
                    last.then_inc(v_free[r], 1)
                if s0 == t0 + tn and quarter == 3:
                    for acc in (b6, b7):
                        last = M(acc[0:m, :], zb[0:1, 0:m], zb[0:1, :], start=False, stop=True)
                    last.then_inc(acc_close, 1)

            pe.wait_ge(const_set, 3)
            for r in range(RV):
                pe.sem_inc(v_free[r], 1)
            run(pe, {"norm": norm, "proj": proj, "pool_mm": pool_mm_, "decay": decay, "heads01": heads01,
                     "heads23": heads23, "state": state, "w_out": w_out, "tok": tok,
                     "query": query, "step": step}, ("proj", "w_out"))


def kernel(**inputs):
    import numpy as np
    import concourse.bacc as bacc
    from concourse.bass_utils import run_bass_kernel_spmd

    a = {k: np.asarray(v) for k, v in inputs.items()}
    f32 = np.float32
    blocks = lambda w: w.reshape(DC, P, -1)
    x = a["x_prompt"][0]
    xcols = np.concatenate([a["meta_tokens"], x[:P], np.zeros((GAP, D), f32), a["x_sample"][0], x[P:]], axis=0)
    xT = xcols.T.reshape(DC, P, COLS).transpose(1, 0, 2)

    def weight_blocks(w):
        return w.reshape(DC, P, -1, P).transpose(2, 1, 0, 3).reshape(-1, P, DC * P)

    slots = [4 * i + h for i in (4, 0, 1, 3, 2) for h in range(4)]
    w_io = np.concatenate([weight_blocks(a["w_in"][0])[slots], weight_blocks(a["w_out"][0])], axis=0)
    order = [(4 * (k >> 1) + r) * 2 + (k & 1) for k in range(4) for r in range(4)]
    subk = a["peer_subkeys"][0].reshape(B_Q, NKEYS, P).transpose(0, 2, 1)
    w_q = np.concatenate([weight_blocks(a["peer_w_query"][0])[order], subk[order]], axis=2)
    fm = lambda v: v.reshape(-1, P).T
    lg = a["hgrn_lb_logits"]
    vecs = np.concatenate([fm(a["norm_mix"][0]), fm(a["norm_ffn"][0]), fm(a["hgrn_out_norm"][0]),
                           fm(a["pool_scale"][0]), fm(lg[0]), fm(lg[1])], axis=1)
    t = np.arange(P)
    masks = np.zeros((P, 8, P), f32)
    masks[:, 0, :] = t[:, None] == t[None, :]
    for l in range(7):
        same = (t[:, None] >> (l + 1)) == (t[None, :] >> (l + 1))
        masks[:, l + 1, :] = same & ((t[:, None] >> l) % 2 == 0) & ((t[None, :] >> l) % 2 == 1)
    small = np.zeros((P, 80), f32)
    small[:, 0:16] = np.arange(16)
    for i, w in enumerate(WINDOWS):
        small[:, 16 + 16 * i:32 + 16 * i] = w / np.minimum(w, np.arange(META) + 1.0)
    arrays = {
        "xT": xT, "w_io": w_io, "w_q": w_q, "pool_w": a["pool_w"][0].transpose(1, 0, 2), "vecs": vecs, "masks": masks,
        "ident": np.eye(P, dtype=f32), "sel": np.tile(np.eye(SAMP, dtype=f32), (4, 1)), "small": small,
        "cacheT": a["cache_pool"][0, 0].T.reshape(4, P, HIST).transpose(1, 0, 2),
        "state": a["state_hgrn"][0, 0].transpose(1, 0, 2), "nf": a["norm_final"],
        "peer_u": a["peer_u"][0], "peer_v": a["peer_v"][0],
    }
    arrays = {k: np.ascontiguousarray(v) for k, v in arrays.items()}
    outs = {"y_prompt": (SEQ, D), "y_sample": (SAMP, D), "sp": (P, 4, P), "ss": (P, 4, P), "cp": (P, 4, HIST),
            "cs": (P, 4, HIST)}
    nc = bacc.Bacc("TRN2", target_bir_lowering=False, num_devices=1)
    args = [nc.dram_tensor("in_" + k, v.shape, FP32, kind="ExternalInput").ap() for k, v in arrays.items()]
    args += [nc.dram_tensor("out_" + k, s, FP32, kind="ExternalOutput").ap() for k, s in outs.items()]
    build(nc, *args)
    r = run_bass_kernel_spmd(nc, [{"in_" + k: v for k, v in arrays.items()}], core_ids=[0]).results[0]
    o = {k: r["out_" + k] for k in outs}
    st = lambda s: s.transpose(1, 0, 2)[None, None]
    hist = lambda c: c.transpose(2, 1, 0).reshape(HIST, 4 * P)[None, None]
    return (o["y_prompt"][None], o["y_sample"][None], st(o["sp"]), hist(o["cp"]), st(o["ss"]), hist(o["cs"]))
```
